# Optimizing a Trainium2 kernel written in Bass

```python
import jax, jax.numpy as jnp
from jax import lax
import numpy as np

D_MODEL = 2048
BATCH = 1
SEQ = 256
DEPTH = 1

N_ATTN_HEADS = 8
ATTN_HEAD_DIM = 128
ATTN_WIDTH = N_ATTN_HEADS * ATTN_HEAD_DIM
Q_BLOCK = 128
LRU_WIDTH = D_MODEL // 2
LRU_BLOCKS = 8
LRU_BLOCK = LRU_WIDTH // LRU_BLOCKS
CONV_WIDTH = 4
LRU_C = 8.0
D_FF = ((8 * D_MODEL // 3 + 255) // 256) * 256
N_MOD = 9
EPS = 1e-6

IN_WIDTHS = (ATTN_WIDTH, ATTN_WIDTH, ATTN_WIDTH, LRU_WIDTH, LRU_WIDTH, D_MODEL, D_MODEL)
IN_TOTAL = sum(IN_WIDTHS)
IN_SPLITS = tuple(int(s) for s in np.cumsum(IN_WIDTHS)[:-1])

kernel_name = "hybrid_stickbreak_rglru_macaron_adaln"

def rms_norm(x, g):
    xf = x.astype(jnp.float32)
    y = xf * lax.rsqrt(jnp.mean(xf * xf, axis=-1, keepdims=True) + EPS)
    return (y * g.astype(jnp.float32)).astype(x.dtype)

def modulate(x, shift, scale):
    return x * (1.0 + scale[:, None, :]) + shift[:, None, :]

def swiglu(x, w_in, w_out):
    gate, up = jnp.split(x @ w_in, 2, axis=-1)
    return (jax.nn.silu(gate) * up) @ w_out

def causal_depthwise_conv(x, w, b):
    y = lax.conv_general_dilated(
        x, w[:, None, :].astype(x.dtype), window_strides=(1,),
        padding=[(CONV_WIDTH - 1, 0)],
        dimension_numbers=("NWC", "WIO", "NWC"),
        feature_group_count=x.shape[-1])
    return y + b

def stick_breaking_attention(q, k, v):
    S = q.shape[2]
    scale = ATTN_HEAD_DIM ** -0.5
    outs = []
    for blk in range(S // Q_BLOCK):
        q0 = blk * Q_BLOCK
        n_keys = q0 + Q_BLOCK
        qb = q[:, :, q0:n_keys]
        kb = k[:, :, :n_keys]
        vb = v[:, :, :n_keys]
        z = jnp.einsum("bhqd,bhkd->bhqk", qb, kb).astype(jnp.float32) * scale
        t_idx = q0 + jnp.arange(Q_BLOCK)[:, None]
        s_idx = jnp.arange(n_keys)[None, :]
        before = s_idx < t_idx
        log_keep = jnp.where(before, jax.nn.log_sigmoid(-z), 0.0)
        rev = lax.cumsum(log_keep, axis=3, reverse=True)
        between = jnp.concatenate([rev[..., 1:], jnp.zeros_like(rev[..., :1])], axis=-1)
        w = jnp.where(before, jnp.exp(jax.nn.log_sigmoid(z) + between), 0.0)
        outs.append(jnp.einsum("bhqk,bhkd->bhqd", w.astype(vb.dtype), vb))
    return jnp.concatenate(outs, axis=2)

def rg_lru(x, w_r, b_r, w_i, b_i, lam):
    B, S, C = x.shape
    xb = x.reshape(B, S, LRU_BLOCKS, LRU_BLOCK)
    r = jax.nn.sigmoid(jnp.einsum("bsnc,ncd->bsnd", xb, w_r).reshape(B, S, C) + b_r)
    i = jax.nn.sigmoid(jnp.einsum("bsnc,ncd->bsnd", xb, w_i).reshape(B, S, C) + b_i)
    log_a = -LRU_C * r.astype(jnp.float32) * jax.nn.softplus(-lam.astype(jnp.float32))
    a = jnp.exp(log_a)
    u = jnp.sqrt(-jnp.expm1(2.0 * log_a)) * (i * x).astype(jnp.float32)

    def combine(left, right):
        a_l, b_l = left
        a_r, b_r2 = right
        return a_l * a_r, a_r * b_l + b_r2

    _, h = lax.associative_scan(combine, (a, u), axis=1)
    return h.astype(x.dtype)

def hybrid_mixer(h, w_in, conv_w, conv_b, w_r, b_r, w_i, b_i, lam, w_br_attn, w_br_lru, w_out):
    B, S, _ = h.shape
    q, k, v, xr, gr, g_attn, g_lru = jnp.split(h @ w_in, IN_SPLITS, axis=-1)

    def heads(t):
        return t.reshape(B, S, N_ATTN_HEADS, ATTN_HEAD_DIM).transpose(0, 2, 1, 3)

    y_attn = stick_breaking_attention(heads(q), heads(k), heads(v))
    y_attn = y_attn.transpose(0, 2, 1, 3).reshape(B, S, ATTN_WIDTH)

    xr = causal_depthwise_conv(xr, conv_w, conv_b)
    y_lru = rg_lru(xr, w_r, b_r, w_i, b_i, lam) * jax.nn.gelu(gr)

    merged = (jax.nn.sigmoid(g_attn) * (y_attn @ w_br_attn)
              + jax.nn.sigmoid(g_lru) * (y_lru @ w_br_lru))
    return merged @ w_out

def setup_inputs(seed: int = 0) -> dict:
    key = jax.random.key(seed)
    ks = jax.random.split(key, 24)
    f32 = jnp.float32

    def nrm(k, shape, std):
        return jax.random.normal(k, shape, f32) * std

    u = jax.random.uniform(ks[13], (DEPTH, LRU_WIDTH), f32, 0.9, 0.999)
    a0 = u ** (1.0 / LRU_C)
    lam = jnp.log(a0) - jnp.log1p(-a0)

    return {
        "x": nrm(ks[0], (BATCH, SEQ, D_MODEL), 1.0),
        "c": nrm(ks[1], (BATCH, D_MODEL), 1.0),
        "w_ada": nrm(ks[2], (DEPTH, D_MODEL, N_MOD * D_MODEL), 0.5 * D_MODEL ** -0.5),
        "b_ada": nrm(ks[3], (DEPTH, N_MOD * D_MODEL), 0.01),
        "norm_ffn1": 1.0 + nrm(ks[4], (DEPTH, D_MODEL), 0.01),
        "w_ffn1_in": nrm(ks[5], (DEPTH, D_MODEL, 2 * D_FF), D_MODEL ** -0.5),
        "w_ffn1_out": nrm(ks[6], (DEPTH, D_FF, D_MODEL), D_FF ** -0.5),
        "norm_mix": 1.0 + nrm(ks[7], (DEPTH, D_MODEL), 0.01),
        "w_in": nrm(ks[8], (DEPTH, D_MODEL, IN_TOTAL), D_MODEL ** -0.5),
        "conv_w": nrm(ks[9], (DEPTH, CONV_WIDTH, LRU_WIDTH), CONV_WIDTH ** -0.5),
        "conv_b": nrm(ks[10], (DEPTH, LRU_WIDTH), 0.01),
        "w_rg_gate": nrm(ks[11], (DEPTH, LRU_BLOCKS, LRU_BLOCK, LRU_BLOCK), LRU_BLOCK ** -0.5),
        "b_rg_gate": nrm(ks[12], (DEPTH, LRU_WIDTH), 0.01),
        "w_in_gate": nrm(ks[14], (DEPTH, LRU_BLOCKS, LRU_BLOCK, LRU_BLOCK), LRU_BLOCK ** -0.5),
        "b_in_gate": nrm(ks[15], (DEPTH, LRU_WIDTH), 0.01),
        "lru_lambda": lam,
        "w_branch_attn": nrm(ks[16], (DEPTH, ATTN_WIDTH, D_MODEL), ATTN_WIDTH ** -0.5),
        "w_branch_lru": nrm(ks[17], (DEPTH, LRU_WIDTH, D_MODEL), LRU_WIDTH ** -0.5),
        "w_out": nrm(ks[18], (DEPTH, D_MODEL, D_MODEL), D_MODEL ** -0.5),
        "norm_ffn2": 1.0 + nrm(ks[19], (DEPTH, D_MODEL), 0.01),
        "w_ffn2_in": nrm(ks[20], (DEPTH, D_MODEL, 2 * D_FF), D_MODEL ** -0.5),
        "w_ffn2_out": nrm(ks[21], (DEPTH, D_FF, D_MODEL), D_FF ** -0.5),
        "norm_final": 1.0 + nrm(ks[22], (D_MODEL,), 0.01),
    }

def reference(x, c, w_ada, b_ada, norm_ffn1, w_ffn1_in, w_ffn1_out, norm_mix, w_in,
              conv_w, conv_b, w_rg_gate, b_rg_gate, w_in_gate, b_in_gate, lru_lambda,
              w_branch_attn, w_branch_lru, w_out, norm_ffn2, w_ffn2_in, w_ffn2_out,
              norm_final):
    h = x
    c_act = jax.nn.silu(c)
    for l in range(DEPTH):
        mod = c_act @ w_ada[l] + b_ada[l]
        sh1, sc1, g1, sh2, sc2, g2, sh3, sc3, g3 = jnp.split(mod, N_MOD, axis=-1)

        y = modulate(rms_norm(h, norm_ffn1[l]), sh1, sc1)
        h = h + 0.5 * g1[:, None, :] * swiglu(y, w_ffn1_in[l], w_ffn1_out[l])

        y = modulate(rms_norm(h, norm_mix[l]), sh2, sc2)
        h = h + g2[:, None, :] * hybrid_mixer(
            y, w_in[l], conv_w[l], conv_b[l], w_rg_gate[l], b_rg_gate[l],
            w_in_gate[l], b_in_gate[l], lru_lambda[l],
            w_branch_attn[l], w_branch_lru[l], w_out[l])

        y = modulate(rms_norm(h, norm_ffn2[l]), sh3, sc3)
        h = h + 0.5 * g3[:, None, :] * swiglu(y, w_ffn2_in[l], w_ffn2_out[l])
    return rms_norm(h, norm_final)


_drawn_inputs = setup_inputs


def setup_inputs(seed=0):
    import zlib

    import numpy as np

    out = dict(_drawn_inputs(seed))
    spreads = {}
    factors = {'b_ada': 5.525,
     'norm_ffn1': 8.0,
     'norm_mix': 8.0,
     'conv_b': 8.0,
     'w_rg_gate': 2.8,
     'b_rg_gate': 64.0,
     'b_in_gate': 59.212,
     'norm_ffn2': 56.606,
     'norm_final': 31.828}
    for name, (base, spread) in spreads.items():
        noise = np.random.default_rng([zlib.crc32(name.encode()), seed]).standard_normal(out[name].shape)
        drawn = base * np.exp(spread * noise) if base else spread * noise
        out[name] = __import__('jax').numpy.asarray(drawn.astype(out[name].dtype))
    for name, factor in factors.items():
        out[name] = (out[name] * factor).astype(out[name].dtype)
    return out
```

```python
from contextlib import ExitStack

import concourse.bass as bass
from concourse import mybir

ALU = mybir.AluOpType
ACT = mybir.ActivationFunctionType
AX = mybir.AxisListType
F32 = mybir.dt.float32
F32R = mybir.dt.float32r
BF16 = mybir.dt.bfloat16

P = 128
COLS = 512
RING = 4
JOB = 1024
MASKED = -1e30


def macaron_layer(nc, x, c, w_ada, b_ada, norm_ffn1, w_ffn1_in, w_ffn1_out, norm_mix, w_in,
                  conv_w, conv_b, w_rg_gate, b_rg_gate, w_in_gate, b_in_gate, lru_lambda,
                  w_branch_attn, w_branch_lru, w_out, norm_ffn2, w_ffn2_in, w_ffn2_out,
                  norm_final, out):
    D = x.shape[2]
    S = x.shape[1]
    TB = S // P
    KT = D // P
    FF = w_ffn1_out.shape[1]
    W = w_branch_attn.shape[1]
    HEADS = W // P
    TAPS = conv_w.shape[1]
    EPS = 1e-6
    SCALE = float(P) ** -0.5
    assert TB == 2 and KT == 16 and FF % COLS == 0 and HEADS == 8 and TAPS == 4

    IN_SUBS = KT // 2
    PAIRS = FF // COLS
    OUT_SUBS = FF // P // 2
    BR_SUBS = HEADS // 2
    N_OUT = D // COLS
    PROJ = 10
    GATES = 2 * N_OUT
    G_FFN = [0, 0]
    G_MIX = PAIRS * 2 * IN_SUBS + N_OUT * OUT_SUBS
    G_GATES = G_MIX + PROJ * IN_SUBS
    G_BR = G_GATES + GATES * IN_SUBS
    G_OUT = G_BR + N_OUT * 2 * BR_SUBS
    G_FFN[1] = G_OUT + N_OUT * IN_SUBS
    assert all(g % RING == 0 for g in (G_MIX, G_GATES, G_BR, G_OUT, G_FFN[1]))

    UNITS = KT
    HEAD_JOBS = [(1, 0), (0, 0), (1, 1), (0, 1)]
    JOBS = [(2, 0), (2, 1), (3, 0), (3, 1), (4, 0), (4, 1), (6, 0), (6, 1), (7, 0), (7, 1),
            (5, 0), (5, 1), (8, 0), (8, 1)]
    UNITS_BEFORE = len(HEAD_JOBS) * UNITS
    HEAD_RING = 8
    LOOP_JOBS = 5

    def units_after(j, window):
        step = {32: 1.75, 28: 1.5, 24: 1.25}[window]
        return [u for u in range(UNITS) if int(u * step) == j]

    def job_col(job):
        mod, half = JOBS[job]
        return mod * D + half * JOB

    def subs(w):
        return w[0].rearrange("(s q p) n -> s p q n", q=2, p=P)

    v_ffn_in = [subs(w_ffn1_in), subs(w_ffn2_in)]
    v_ffn_out = [subs(w_ffn1_out), subs(w_ffn2_out)]
    v_in, v_attn, v_lru, v_out = subs(w_in), subs(w_branch_attn), subs(w_branch_lru), subs(w_out)
    v_ada = w_ada[0].rearrange("(p k) n -> p k n", k=UNITS)
    v_bada = b_ada.rearrange("a (m n) -> a m n", m=9)
    proj_col = [3 * W + COLS * i for i in range(4)] + [COLS * i for i in range(6)]
    gates_col = 5 * W

    ctx = ExitStack()
    with ctx:
        def sb(name, shape, dt=F32):
            return ctx.enter_context(nc.sbuf_tensor(name, shape, dt))

        def sem(name):
            return ctx.enter_context(nc.semaphore(name))

        resid = sb("resid", [P, TB, D])
        w_raw = sb("w_raw", [P, RING, 2 * COLS])
        w_hi = sb("w_hi", [P, RING, 2 * COLS], F32R)
        w_lo = sb("w_lo", [P, RING, 2 * COLS], F32R)
        ada_ring = sb("ada_ring", [P, 2, JOB])
        acc = sb("acc", [P, JOB])
        mod_row = sb("mod_row", [P, JOB])
        gate_row = sb("gate_row", [P, D])
        stage = sb("stage", [P, TB * COLS])
        tm = sb("tm", [P, TB * COLS])
        ident = sb("ident", [P, P])
        ident_bf = sb("ident_bf", [P, P], BF16)
        unseen = sb("unseen", [P, 3 * P], BF16)
        bar = sb("bar", [P, 3 * P], BF16)
        ones = sb("ones", [P, 1])
        spare = sb("spare", [P, 2])
        ccol = sb("ccol", [P, UNITS])
        colA = sb("colA", [P, 112])
        colB = sb("colB", [P, 96])
        mods = sb("mods", [P, 6, KT])
        ssq = sb("ssq", [P, TB, 4])
        stat = sb("stat", [P, 4, TB])
        sp = sb("sp", [P, 8, HEADS])
        rowsA, rowsB = mod_row[0:112, 0:P], mod_row[0:96, P:2 * P]
        GAIN, SHIFT = [0, 2, 4], [1, 3, 5]
        mod_at = {1: 0, 0: 1, 4: 2, 3: 3, 7: 4, 6: 5}

        def region(*tensors):
            with ExitStack() as r:
                return [r.enter_context(nc.sbuf_tensor(n, s, d)) for n, s, d in tensors]

        final_gain, = region(("final_gain", [P, D], F32))
        act_hi = sb("act_hi", [P, KT, S], F32R)
        act_lo = sb("act_lo", [P, KT, S], F32R)

        head_ring, head_acc, x_turned, xn_h = region(
            ("head_ring", [P, HEAD_RING, JOB], F32), ("head_acc", [P, 4, JOB], F32),
            ("x_turned", [P, KT, S], F32), ("xn_h", [P, TB, D], F32))
        xn, = region(("xn", [P, TB, D], F32))
        q_t, k_t, v_tok, ylru_hi, ylru_lo, sg_merge, xr_t, gr_t = region(
            ("q_t", [P, HEADS, S], F32), ("k_t", [P, HEADS, S], F32),
            ("v_tok", [P, TB, W], F32), ("ylru_hi", [P, HEADS, S], F32R),
            ("ylru_lo", [P, HEADS, S], F32R), ("sg_merge", [P, GATES, TB * COLS], F32),
            ("xr_t", [P, HEADS, S], F32), ("gr_t", [P, HEADS, S], F32))
        yat_hi, yat_lo, _, xc, lru_r, lru_i, lru_t, q_one, v_one, w_turned = region(
            ("yat_hi", [P, HEADS, S], F32R), ("yat_lo", [P, HEADS, S], F32R),
            ("gap", [P, 3, HEADS * S], F32), ("xc", [P, HEADS, S], F32),
            ("lru_r", [P, HEADS, S], F32), ("lru_i", [P, HEADS, S], F32),
            ("lru_t", [P, HEADS, S], F32), ("q_one", [P, S], F32),
            ("v_one", [P, TB, P], F32), ("w_turned", [P, 3 * P], F32))
        hid_hi = sb("hid_hi", [P, FF // P, S], F32R)
        hid_lo = sb("hid_lo", [P, FF // P, S], F32R)
        ps = ctx.enter_context(nc.psum_tensor("ps", [P, 8, COLS], F32))
        w_gate_r = gate_row[:, 0:HEADS * P].rearrange("p (n d) -> p n d", n=HEADS)
        w_gate_i = gate_row[:, HEADS * P:].rearrange("p (n d) -> p n d", n=HEADS)

        A_NORM = [0, 16, 32]
        A_BIAS = {1: 48, 0: 64, 4: 80, 3: 96}
        B_TAP, B_CONVB, B_BR, B_BI, B_LAM = 0, 32, 40, 48, 56
        B_BIAS = {7: 64, 6: 80}

        SMALLS = len(A_NORM) + len(A_BIAS) + 5 + len(B_BIAS)

        def bias_cols(mod, half):
            t, at = (colA, A_BIAS[mod]) if mod in A_BIAS else (colB, B_BIAS[mod])
            return t[:, at + 8 * half:at + 8 * half + 8]

        small_landed = sem("small_landed")
        c_landed = sem("c_landed")
        x_landed = [sem(f"x_landed{t}") for t in range(TB)]
        head_landed = [sem(f"head_landed{i}") for i in range(HEAD_RING)]
        w_landed = [sem(f"w_landed{i}") for i in range(RING)]
        ada_landed = [sem(f"ada_landed{i}") for i in range(2)]
        bias_landed = sem("bias_landed")
        lru_w_landed = sem("lru_w_landed")
        gain_landed = sem("gain_landed")
        stored = sem("stored")
        hi_rounded = sem("hi_rounded")
        lo_split = sem("lo_split")
        sub_multiplied = sem("sub_multiplied")
        unit_added = sem("unit_added")
        acc_free = sem("acc_free")
        mods_made = sem("mods_made")
        pool_step = sem("pool_step")
        consts_made = sem("consts_made")
        dve_step = sem("dve_step")
        c_ready = sem("c_ready")
        rows_turned = sem("rows_turned")
        cols_ready = sem("cols_ready")
        job_summed = sem("job_summed")
        squared = sem("squared")
        ms_ready = sem("ms_ready")
        rstd_ready = sem("rstd_ready")
        xn_ready = sem("xn_ready")
        xn_turned = sem("xn_turned")
        x_kept = sem("x_kept")
        y_ready = sem("y_ready")
        y_hi = sem("y_hi")
        y_lo = sem("y_lo")
        silu_done = sem("silu_done")
        tm_written = sem("tm_written")
        turned = sem("turned")
        turn_hi = sem("turn_hi")
        turn_lo = sem("turn_lo")
        turn_kept = sem("turn_kept")
        resid_added = sem("resid_added")
        kept = sem("kept")
        conv_done = sem("conv_done")
        gates_summed = sem("gates_summed")
        gates_done = sem("gates_done")
        decay_done = sem("decay_done")
        root_in = sem("root_in")
        root_done = sem("root_done")
        ylru_ready = sem("ylru_ready")
        ylru_hi_done = sem("ylru_hi_done")
        ylru_lo_done = sem("ylru_lo_done")
        lam_abs = sem("lam_abs")
        lam_exp = sem("lam_exp")
        head_fetched = sem("head_fetched")
        scores = sem("scores")
        betas = sem("betas")
        scanned = sem("scanned")
        weights_ready = sem("weights_ready")
        weights_turned = sem("weights_turned")
        weights_kept = sem("weights_kept")
        head_out = sem("head_out")
        yat_hi_done = sem("yat_hi_done")
        attn_split = sem("attn_split")
        attn_merged = sem("attn_merged")
        lru_merged = sem("lru_merged")
        out_ready = sem("out_ready")

        T_FFN = [0, PAIRS + 8 + N_OUT]
        T_MIX = PAIRS
        T_BR = PAIRS + 8
        L_FFN = [0, PAIRS + N_OUT]
        L_BR = PAIRS
        R_FFN, R_OUT = [0, 2 * N_OUT], N_OUT
        job0_of = {"ffn_out": LOOP_JOBS, "proj": 8, "br": 11, "ffn2": 12}

        PIECES = IN_SUBS

        def y_space(q):
            return (stage, tm)[q // 2 % 2][:, (q % 2) * 2 * S:(q % 2 + 1) * 2 * S].rearrange("p (k s) -> p k s", s=S)

        def sqs(stage_no):
            return 8 * stage_no

        block = ctx.enter_context(nc.Block())

        @block.sync
        def _(sp_):
            def load_w(view, s, col, g, j, first=False):
                if not first:
                    sp_.wait_ge(lo_split, g - RING + 1)
                sp_.dma_start(w_raw[:, j % RING, :].rearrange("p (q n) -> p q n", q=2),
                              view[s, :, :, bass.ds(col, COLS)]).then_inc(w_landed[j % RING], 16)

            def load_unit(col, n, u, at=None):
                sp_.wait_ge(unit_added, n - 1)
                src = v_ada[:, u, bass.ds(col, JOB)] if at is None else \
                    v_ada[:, bass.ds(at, 1), bass.ds(col, JOB)].rearrange("p a n -> p (a n)")
                sp_.dma_start(ada_ring[:, u % 2, :], src).then_inc(ada_landed[u % 2], 16)

            def load_bias(job):
                mod, half = JOBS[job]
                sp_.dma_start(gate_row[0:1, half * JOB:(half + 1) * JOB],
                              v_bada[:, mod, half * JOB:(half + 1) * JOB]).then_inc(bias_landed, 16)

            sp_.dma_start(ccol[:, :], c[0].rearrange("(p k) -> p k", k=UNITS)).then_inc(c_landed, 16)
            x_v = x[0].rearrange("(t p) d -> t p d", p=P)
            for t in range(TB):
                sp_.dma_start(resid[:, t, :], x_v[t]).then_inc(x_landed[t], 16)
            smalls = [(rowsA[at:at + KT, :], src[0].rearrange("(k p) -> k p", p=P))
                      for at, src in zip(A_NORM, (norm_ffn1, norm_mix, norm_ffn2))]
            smalls += [(rowsA[at:at + KT, :], v_bada[0, mod, :].rearrange("(k p) -> k p", p=P))
                       for mod, at in A_BIAS.items()]
            smalls += [(rowsB[B_TAP:B_TAP + HEADS * TAPS, :], conv_w[0].rearrange("j (k p) -> (j k) p", p=P))]
            smalls += [(rowsB[at:at + HEADS, :], src[0].rearrange("(k p) -> k p", p=P))
                       for at, src in ((B_CONVB, conv_b), (B_BR, b_rg_gate), (B_BI, b_in_gate), (B_LAM, lru_lambda))]
            smalls += [(rowsB[at:at + KT, :], v_bada[0, mod, :].rearrange("(k p) -> k p", p=P))
                       for mod, at in B_BIAS.items()]
            assert len(smalls) == SMALLS
            for job, (mod, half) in enumerate(HEAD_JOBS):
                for u in range(UNITS):
                    n = job * UNITS + u
                    if n >= HEAD_RING:
                        sp_.wait_ge(unit_added, n - HEAD_RING + 1)
                    sp_.dma_start(head_ring[:, n % HEAD_RING, :],
                                  v_ada[:, u, mod * D + half * JOB:mod * D + (half + 1) * JOB])\
                       .then_inc(head_landed[n % HEAD_RING], 16)
                    if n < SMALLS:
                        sp_.dma_start(*smalls[n]).then_inc(small_landed, 16)

            def ffn(f):
                g0 = G_FFN[f]
                for j in range(IN_SUBS):
                    load_w(v_ffn_in[f], j, 0, g0 + j, j, first=(g0 + j < RING))
                if f == 0:
                    load_bias(0)
                    load_bias(1)
                else:
                    sp_.wait_ge(resid_added, TB * (R_OUT + N_OUT))
                    load_bias(12)
                    load_bias(13)

                def pairs(lo, hi, job0):
                    with sp_.Fori(lo, hi) as b:
                        for j in range(4 * IN_SUBS):
                            ch = j // IN_SUBS
                            col = b * (2 * COLS) + [FF, COLS, FF + COLS, 2 * COLS][ch]
                            load_w(v_ffn_in[f], j % IN_SUBS, col, g0 + IN_SUBS + b * (4 * IN_SUBS) + j, j)
                            if job0 is not None:
                                for u in units_after(j, 32):
                                    load_unit(b * JOB + job_col(job0), b * UNITS + UNITS_BEFORE + job0 * UNITS + u, u)

                if f == 0:
                    pairs(0, LOOP_JOBS, 0)
                else:
                    pairs(0, 2, job0_of["ffn2"])
                    pairs(2, 5, None)
                g = g0 + IN_SUBS * (2 * PAIRS - 1)
                for j in range(IN_SUBS):
                    load_w(v_ffn_in[f], j, FF + (PAIRS - 1) * COLS, g + j, j)
                g += IN_SUBS
                for i in range(N_OUT * OUT_SUBS):
                    n, j = divmod(i, OUT_SUBS)
                    load_w(v_ffn_out[f], j, n * COLS, g + i, i)
                    if f == 0 and i < 3 * 28:
                        job = job0_of["ffn_out"] + i // 28
                        for u in units_after(i % 28, 28):
                            load_unit(job_col(job), UNITS_BEFORE + job * UNITS + u, u)

            ffn(0)
            for ch in range(PROJ):
                for j in range(IN_SUBS):
                    i = ch * IN_SUBS + j
                    load_w(v_in, j, proj_col[ch], G_MIX + i, i)
                    if i == 2 * RING:
                        sp_.wait_ge(resid_added, TB * N_OUT)
                        for dst, src in ((w_gate_r, w_rg_gate), (w_gate_i, w_in_gate)):
                            sp_.dma_start(dst, src[0].rearrange("n c d -> c n d")).then_inc(lru_w_landed, 16)
                    for u in units_after((i - IN_SUBS) % 32, 32) if ch in range(1, 9) else ():
                        job = job0_of["proj"] + (i - IN_SUBS) // 32
                        load_unit(job_col(job), UNITS_BEFORE + job * UNITS + u, u)
            sp_.wait_ge(gates_done, HEADS)
            load_bias(10)
            load_bias(11)
            n10 = UNITS_BEFORE + 10 * UNITS
            for j in range(IN_SUBS):
                load_w(v_in, j, gates_col, G_GATES + j, j)
                if j % 2:
                    load_unit(job_col(10), n10 + j // 2, j // 2)
            with sp_.Fori(0, (GATES - 2) // 2) as b:
                for j in range(2 * IN_SUBS):
                    load_w(v_in, j % IN_SUBS, b * (2 * COLS) + gates_col + COLS * (1 + j // IN_SUBS),
                           G_GATES + IN_SUBS + b * (2 * IN_SUBS) + j, j)
                    if j % 4 == 3:
                        load_unit(job_col(10), b * 4 + (n10 + 4 + j // 4), j // 4, at=b * 4 + (4 + j // 4))
            for j in range(IN_SUBS):
                load_w(v_in, j, gates_col + COLS * (GATES - 1), G_GATES + IN_SUBS * (GATES - 1) + j, j)
            for i in range(N_OUT * 2 * BR_SUBS):
                n, j = divmod(i, 2 * BR_SUBS)
                load_w(v_attn if j < BR_SUBS else v_lru, j % BR_SUBS, n * COLS, G_BR + i, i)
                for u in units_after(i, 32):
                    load_unit(job_col(11), UNITS_BEFORE + 11 * UNITS + u, u)
            for i in range(N_OUT * IN_SUBS):
                n, j = divmod(i, IN_SUBS)
                load_w(v_out, j, n * COLS, G_OUT + i, i)
            ffn(1)
            sp_.wait_ge(sub_multiplied, G_FFN[1] + 2 * PAIRS * IN_SUBS)
            sp_.dma_start(final_gain[:, :], norm_final.rearrange("(a d) -> a d", a=1)
                          .to_broadcast([P, D])).then_inc(gain_landed, 16)
            out_v = out[0].rearrange("(t p) d -> p t d", p=P)
            for n in range(2 * N_OUT):
                t, q = n % TB, n // TB
                sp_.wait_ge(out_ready, n + 1)
                sp_.dma_start(out_v[:, t, q * COLS:(q + 1) * COLS],
                              resid[:, t, q * COLS:(q + 1) * COLS]).then_inc(stored, 16)
            sp_.wait_ge(stored, 16 * 2 * N_OUT)

        @block.gpsimd
        def _(pool):
            n_step = [0]

            def step(ins):
                n_step[0] += 1
                ins.then_inc(pool_step, 1)
                pool.wait_ge(pool_step, n_step[0])

            step(pool.memset(ident[:, :], 0.0))
            step(pool.memset(unseen[:, :], 0.0))
            step(pool.memset(bar[:, :], 0.0))
            pool.memset(ones[:, :], 1.0).then_inc(consts_made, 1)
            pool.affine_select(out=ident[:, :], in_=ident[:, :], compare_op=ALU.not_equal, fill=1.0,
                               base=0, pattern=[[-1, P]], channel_multiplier=1).then_inc(consts_made, 1)
            for m, fill in ((unseen, 1.0), (bar, MASKED)):
                for b in (0, 2):
                    pool.affine_select(out=m[:, b * P:(b + 1) * P], in_=m[:, b * P:(b + 1) * P],
                                       compare_op=ALU.is_gt, fill=fill, base=0, pattern=[[-1, P]],
                                       channel_multiplier=1).then_inc(consts_made, 1)
            pool.wait_ge(consts_made, 6)
            pool.tensor_copy(ident_bf[:, :], ident[:, :]).then_inc(consts_made, 1)
            pool.memset(spare[:, 0:1], 0.0).then_inc(acc_free, 1)

            def finish_job(job):
                mod, half = JOBS[job]
                pool.wait_ge(unit_added, UNITS_BEFORE + (job + 1) * UNITS)
                if job:
                    pool.wait_ge(mods_made, job)
                if mod in (2, 5, 8):
                    row = gate_row[:, half * JOB:(half + 1) * JOB]
                    pool.wait_ge(bias_landed, 16 * (2 if mod == 2 else 4 if mod == 5 else 6))
                    step(pool.tensor_tensor(acc[0:1, :], acc[0:1, :], row[0:1, :], ALU.add))
                    pool.partition_all_reduce(row, acc[:, :], P, bass.bass_isa.ReduceOp.add).then_inc(acc_free, 1)
                    pool.wait_ge(acc_free, job + 2)
                    pool.memset(spare[:, 0:1], 0.0).then_inc(mods_made, 1)
                    return
                pool.partition_all_reduce(mod_row[:, :], acc[:, :], P, bass.bass_isa.ReduceOp.add).then_inc(acc_free, 1)
                pool.wait_ge(acc_free, job + 2)
                blocks = mod_row[:, :].rearrange("p (b f) -> p b f", f=P)
                step(pool.tensor_tensor(blocks, blocks, ident[:, None, :].to_broadcast([P, 8, P]), ALU.mult))
                w = P // 2
                while w:
                    step(pool.tensor_tensor(blocks[:, :, 0:w], blocks[:, :, 0:w], blocks[:, :, w:2 * w], ALU.add))
                    w //= 2
                col = mods[:, mod_at[mod], 8 * half:8 * half + 8]
                if mod in (4, 7):
                    gain = A_NORM[1 if mod == 4 else 2] + 8 * half
                    step(pool.tensor_tensor(col, blocks[:, :, 0], bias_cols(mod, half), ALU.add))
                    step(pool.tensor_scalar(col, col, 1.0, None, ALU.add))
                    pool.tensor_tensor(col, col, colA[:, gain:gain + 8], ALU.mult).then_inc(mods_made, 1)
                else:
                    pool.tensor_tensor(col, blocks[:, :, 0], bias_cols(mod, half), ALU.add).then_inc(mods_made, 1)

            def fetch_head(h):
                pool.tensor_copy(q_one[:, :], q_t[:, bass.ds(h, 1), :].rearrange("p a s -> p (a s)")).then_inc(head_fetched, 1)
                pool.tensor_copy(v_one[:, :, :], v_tok[:, :, bass.ds(h * P, P)]).then_inc(head_fetched, 1)

            pool.wait_ge(cols_ready, 1)
            for job in range(10):
                finish_job(job)
            pool.wait_ge(turn_kept, 8)
            pool.wait_ge(kept, 2)
            pool.wait_ge(ylru_ready, HEADS)
            fetch_head(0)
            with pool.Fori(1, HEADS) as h:
                pool.wait_ge(head_out, h)
                fetch_head(h)
            for job in range(10, len(JOBS)):
                finish_job(job)

        @block.scalar
        def _(act):
            def round_hi(g, j, first=False):
                act.wait_ge(w_landed[j % RING], (g - j) * (16 // RING) + 16 * (j // RING + 1))
                if not first:
                    act.wait_ge(sub_multiplied, g - RING + 1)
                act.copy(w_hi[:, j % RING, :], w_raw[:, j % RING, :]).then_inc(hi_rounded, 1)

            def square(stage_no, i, t, n):
                if sqs(stage_no) + i:
                    act.wait_ge(squared, sqs(stage_no) + i)
                act.activation(tm[:, 0:COLS], resid[:, t, n * COLS:(n + 1) * COLS], ACT.Square,
                               accum_out=ssq[:, t, n:n + 1]).then_inc(squared, 1)

            def square_chunk(stage_no, n, r0):
                for t in range(TB):
                    act.wait_ge(resid_added, TB * (r0 + n) + t + 1)
                    square(stage_no, TB * n + t, t, n)

            def rstd(stage_no):
                act.wait_ge(ms_ready, stage_no + 1)
                act.activation(stat[:, 3, :], stat[:, 2, :], ACT.Sqrt).then_inc(rstd_ready, 1)

            def round_y(stage_no, q):
                act.wait_ge(y_ready, PIECES * stage_no + q + 1)
                act.copy(act_hi[:, 2 * q:2 * q + 2, :], y_space(q)).then_inc(y_hi, 1)

            def round_turned(dst, k, count):
                act.wait_ge(turned, count)
                act.copy(dst[:, bass.ds(k, 4), :], ps[:, 4:6, :].rearrange("p b (k s) -> p (b k) s", s=S)).then_inc(turn_hi, 1)

            act.wait_ge(c_landed, 16)
            act.activation(ccol[:, :], ccol[:, :], ACT.Silu).then_inc(c_ready, 1)
            for t in range(TB):
                act.wait_ge(x_landed[t], 16)
                for n in range(4):
                    square(0, 4 * t + n, t, n)
            rstd(0)
            for q in range(PIECES):
                act.wait_ge(xn_turned, q + 1)
                act.copy(x_turned[:, 2 * q:2 * q + 2, :], ps[:, q, :].rearrange("p (k s) -> p k s", s=S)).then_inc(x_kept, 1)
            act.wait_ge(lam_abs, 1)
            act.activation(sp[:, 1, :], sp[:, 0, :], ACT.Exp, scale=-1.0).then_inc(lam_exp, 1)

            def ffn(f):
                g0, t0 = G_FFN[f], T_FFN[f]
                if f == 0:
                    for j in range(RING):
                        round_hi(g0 + j, j, first=True)
                    for q in range(PIECES):
                        round_y(0, q)
                    for j in range(RING, IN_SUBS):
                        round_hi(g0 + j, j)
                else:
                    behind_norm(g0, R_OUT, 2)

                def silu(g, n):
                    act.wait_ge(sub_multiplied, g)
                    act.activation(stage[:, :], ps[:, 0:2, :], ACT.Silu).then_inc(silu_done, 1)

                with act.Fori(0, PAIRS - 1) as i:
                    g = g0 + IN_SUBS + i * (2 * IN_SUBS)
                    for j in range(IN_SUBS):
                        round_hi(g + j, j)
                        if j == 2:
                            silu(g, i)
                    for j in range(IN_SUBS, 2 * IN_SUBS):
                        round_hi(g + j, j)
                        if j == IN_SUBS + 4:
                            round_turned(hid_hi, i * 4, t0 + 1 + i)
                g = g0 + IN_SUBS * (2 * PAIRS - 1)
                for j in range(IN_SUBS):
                    round_hi(g + j, j)
                    if j == 2:
                        silu(g, PAIRS - 1)
                g += IN_SUBS
                for i in range(N_OUT * OUT_SUBS):
                    n, j = divmod(i, OUT_SUBS)
                    round_hi(g + i, i)
                    if i == 4:
                        round_turned(hid_hi, 4 * (PAIRS - 1), t0 + PAIRS)
                    if j == 3 and n:
                        square_chunk(1 if f == 0 else 3, n - 1, R_FFN[f])

            def last_chunk(r0, stage_no):
                act.activation(spare[:, 1:2], stat[:, 3, 0:1], ACT.Sqrt)
                square_chunk(stage_no, N_OUT - 1, r0)
                rstd(stage_no)

            def behind_norm(g, r0, stage_no):
                for j in range(RING - 1):
                    round_hi(g + j, j)
                last_chunk(r0, stage_no)
                for q in range(3):
                    round_y(stage_no, q)
                round_hi(g + RING - 1, RING - 1)
                for q in range(3, PIECES):
                    round_y(stage_no, q)
                for j in range(RING, IN_SUBS):
                    round_hi(g + j, j)

            ffn(0)

            def lru_gate(b):
                act.wait_ge(gates_summed, b + 1)
                bank = ps[:, 6 + b % 2, :]
                act.activation(lru_r[:, b, :], bank[:, 0:S], ACT.Sigmoid, bias=colB[:, B_BR + b:B_BR + b + 1])
                act.activation(lru_i[:, b, :], bank[:, S:2 * S], ACT.Sigmoid,
                               bias=colB[:, B_BI + b:B_BI + b + 1]).then_inc(gates_done, 1)

            def lru_decay(b):
                if b == 0:
                    act.wait_ge(gates_done, HEADS)
                act.activation(lru_t[:, b, :], lru_r[:, b, :], ACT.Tanh, scale=sp[:, 6, b:b + 1]).then_inc(decay_done, 1)
                act.activation(lru_r[:, b, :], lru_r[:, b, :], ACT.Exp, scale=sp[:, 7, b:b + 1]).then_inc(decay_done, 1)

            for ch in range(PROJ):
                for j in range(IN_SUBS):
                    i = ch * IN_SUBS + j
                    if i == 0:
                        behind_norm(G_MIX, R_FFN[0], 1)
                    elif ch:
                        round_hi(G_MIX + i, i)
                    if ch == 9 and j == 2:
                        act.wait_ge(sub_multiplied, G_MIX + 9 * IN_SUBS)
                        act.copy(v_tok[:, :, 0:COLS], ps[:, 0:2, :]).then_inc(kept, 1)
                    if j == 4 and 1 <= ch <= 8:
                        d = (xr_t, gr_t, q_t, k_t)[(ch - 1) // 2][:, 4 * ((ch - 1) % 2):4 * ((ch - 1) % 2) + 4, :]
                        act.wait_ge(turned, T_MIX + ch)
                        act.activation(d, ps[:, 4:6, :].rearrange("p b (k s) -> p (b k) s", s=S),
                                       ACT.Gelu_apprx_tanh if ch in (3, 4) else ACT.Copy).then_inc(turn_kept, 1)
                    if ch == 4 and j >= RING:
                        lru_gate(j - RING)
                    if ch == 5 and j < RING:
                        lru_gate(j + RING)
                    if ch == 6:
                        lru_decay(j)
                    if ch == 7 and j == 7:
                        act.wait_ge(root_in, 2)
                        act.activation(lru_t[:, :, :], lru_t[:, :, :], ACT.Sqrt).then_inc(root_done, 1)
                    if ch == 9 and j == 1:
                        act.wait_ge(ylru_ready, 4)
                        act.copy(ylru_hi[:, 0:4, :], lru_t[:, 0:4, :]).then_inc(ylru_hi_done, 1)

            def gate_chunk(cc, g, s, first=False):
                for j in range(IN_SUBS):
                    round_hi(g + j, j)
                    if j == 0 and first:
                        act.wait_ge(ylru_ready, HEADS)
                        act.copy(ylru_hi[:, 4:8, :], lru_t[:, 4:8, :]).then_inc(ylru_hi_done, 1)
                    if j == 2:
                        act.wait_ge(sub_multiplied, g)
                        if first:
                            act.copy(v_tok[:, :, COLS:2 * COLS], ps[:, 2:4, :]).then_inc(kept, 1)
                        else:
                            keep_gate(cc - 1, s)
                    if j == 3:
                        act.wait_ge(scores, cc + 1)
                        z = ps[:, 6, 0:3 * P]
                        act.activation(stage[:, 0:3 * P], z, ACT.Sigmoid, scale=SCALE)
                        act.activation(stage[:, COLS:COLS + 3 * P], z, ACT.Sigmoid, scale=-SCALE).then_inc(betas, 1)
                act.wait_ge(weights_turned, cc + 1)
                act.copy(w_turned[:, :], ps[:, 4, 0:3 * P]).then_inc(weights_kept, 1)
                act.wait_ge(head_out, cc + 1)
                act.copy(yat_hi[:, bass.ds(cc, 1), :].rearrange("p a s -> p (a s)"), ps[:, 5, 0:S]).then_inc(yat_hi_done, 1)

            def keep_gate(cc, s):
                act.activation(sg_merge[:, bass.ds(cc, 1), :].rearrange("p a n -> p (a n)"),
                               ps[:, s:s + 2, :], ACT.Sigmoid).then_inc(kept, 1)

            gate_chunk(0, G_GATES, 2, first=True)
            act.wait_ge(ylru_lo_done, 2)
            with act.Fori(0, (GATES - 2) // 2) as b:
                for half in range(2):
                    gate_chunk(b * 2 + 1 + half, G_GATES + IN_SUBS * (1 + half) + b * (2 * IN_SUBS), 2 * half)
            gate_chunk(GATES - 1, G_GATES + IN_SUBS * (GATES - 1), 0)

            for j in range(BR_SUBS):
                round_hi(G_BR + j, j)
                if j == 2:
                    act.wait_ge(sub_multiplied, G_BR)
                    keep_gate(GATES - 1, 2)
            with act.Fori(0, N_OUT - 1) as n:
                g = G_BR + BR_SUBS + n * (2 * BR_SUBS)
                for j in range(2 * BR_SUBS):
                    round_hi(g + j, j)
                round_turned(act_hi, n * 4, T_BR + 1 + n)
            for j in range(BR_SUBS):
                round_hi(G_OUT - BR_SUBS + j, j)
            for i in range(N_OUT * IN_SUBS):
                n, j = divmod(i, IN_SUBS)
                round_hi(G_OUT + i, i)
                if i == 4:
                    round_turned(act_hi, 4 * (N_OUT - 1), T_BR + N_OUT)
                if j == 3 and n:
                    square_chunk(2, n - 1, R_OUT)
            ffn(1)
            last_chunk(R_FFN[1], 3)

        @block.vector
        def _(dve):
            n_step = [0]

            def step(ins, wait=True):
                n_step[0] += 1
                ins.then_inc(dve_step, 1)
                if wait:
                    dve.wait_ge(dve_step, n_step[0])

            def split_lo(g, j):
                dve.wait_ge(hi_rounded, g + 1)
                dve.tensor_tensor(w_lo[:, j % RING, :], w_raw[:, j % RING, :],
                                  w_hi[:, j % RING, :].bitcast(F32), ALU.subtract).then_inc(lo_split, 1)

            def add_unit(n, u, dst, src, landed, count, jobs_before=None):
                dve.wait_ge(landed, count)
                if u == 0:
                    if jobs_before is not None:
                        dve.wait_ge(acc_free, jobs_before + 1)
                    dve.tensor_scalar(dst, src, ccol[:, 0:1], None, ALU.mult).then_inc(unit_added, 1)
                else:
                    dve.wait_ge(unit_added, n)
                    dve.scalar_tensor_tensor(out=dst, in0=src, scalar=ccol[:, u:u + 1], in1=dst,
                                             op0=ALU.mult, op1=ALU.add).then_inc(unit_added, 1)

            def job_unit(job, u):
                add_unit(job * UNITS + (UNITS_BEFORE + u), u, acc[:, :], ada_ring[:, u % 2, :],
                         ada_landed[u % 2], job * (16 * UNITS // 2) + 16 * (u // 2 + 1), jobs_before=job)

            def job_unit_at(job, b, u):
                dve.wait_ge(ada_landed[u % 2], b * 32 + 16 * (job * UNITS // 2 + u // 2 + 1))
                dve.wait_ge(unit_added, b * 4 + (UNITS_BEFORE + job * UNITS + u))
                dve.scalar_tensor_tensor(out=acc[:, :], in0=ada_ring[:, u % 2, :], scalar=ccol[:, bass.ds(b * 4 + u, 1)],
                                         in1=acc[:, :], op0=ALU.mult, op1=ALU.add).then_inc(unit_added, 1)

            def mean_square(stage_no):
                dve.wait_ge(squared, sqs(stage_no + 1))
                step(dve.tensor_reduce(stat[:, 0, :], ssq[:, :, :], AX.X, ALU.add))
                step(dve.tensor_scalar(stat[:, 1, :], stat[:, 0, :], 1.0 / D, EPS, ALU.mult, ALU.add))
                dve.reciprocal(stat[:, 2, :], stat[:, 1, :]).then_inc(ms_ready, 1)
                dve.wait_ge(rstd_ready, stage_no + 1)

            def norm_piece(stage_no, q, dst):
                cols = slice(q * 2 * P, (q + 1) * 2 * P)
                for t in range(TB):
                    ins = dve.tensor_scalar(dst[:, t, cols], resid[:, t, cols], stat[:, 3, t:t + 1], None, ALU.mult)
                ins.then_inc(xn_ready, 1)

            def y_piece(stage_no, q):
                if q >= 4:
                    dve.wait_ge(y_lo, PIECES * stage_no + q - 3)
                if stage_no == 0:
                    src = x_turned[:, 2 * q:2 * q + 2, :]
                    dve.wait_ge(x_kept, PIECES)
                else:
                    src = ps[:, q, :].rearrange("p (k s) -> p k s", s=S)
                    dve.wait_ge(xn_turned, PIECES * stage_no + q + 1)
                for k in range(2):
                    ins = dve.tensor_scalar(y_space(q)[:, k, :], src[:, k, :],
                                            mods[:, GAIN[stage_no], 2 * q + k:2 * q + k + 1],
                                            mods[:, SHIFT[stage_no], 2 * q + k:2 * q + k + 1], ALU.mult, ALU.add)
                ins.then_inc(y_ready, 1)

            def y_low(stage_no, q):
                dve.wait_ge(y_hi, PIECES * stage_no + q + 1)
                dve.tensor_tensor(act_lo[:, 2 * q:2 * q + 2, :], y_space(q),
                                  act_hi[:, 2 * q:2 * q + 2, :].bitcast(F32), ALU.subtract).then_inc(y_lo, 1)

            def split_turned(hi, lo, k, count):
                dve.wait_ge(turn_hi, count)
                dve.tensor_tensor(lo[:, bass.ds(k, 4), :], ps[:, 4:6, :].rearrange("p b (k s) -> p (b k) s", s=S),
                                  hi[:, bass.ds(k, 4), :].bitcast(F32), ALU.subtract).then_inc(turn_lo, 1)

            def add_resid(n, g_end, half):
                dve.wait_ge(sub_multiplied, g_end)
                for t in range(TB):
                    prod = stage[:, t * COLS:(t + 1) * COLS]
                    r = resid[:, t, n * COLS:(n + 1) * COLS]
                    step(dve.scalar_tensor_tensor(out=prod, in0=ps[:, 2 * (n % 2) + t, :], scalar=half,
                                                  in1=gate_row[:, n * COLS:(n + 1) * COLS],
                                                  op0=ALU.mult, op1=ALU.mult))
                    dve.tensor_tensor(r, r, prod, ALU.add).then_inc(resid_added, 1)

            def parameters():
                dve.wait_ge(rows_turned, 1)
                step(dve.tensor_copy(colA[:, :], ps[:, 0, 0:112]), wait=False)
                step(dve.tensor_copy(colB[:, :], ps[:, 0, 128:224]))
                dve.memset(sp[:, 2, :], 0.0).then_inc(cols_ready, 1)
                lam = colB[:, B_LAM:B_LAM + HEADS]
                dve.scalar_tensor_tensor(out=sp[:, 0, :], in0=lam, scalar=-1.0, in1=lam,
                                         op0=ALU.mult, op1=ALU.max).then_inc(lam_abs, 1)
                dve.wait_ge(lam_exp, 1)
                e, s1, s2, pw, q_ = sp[:, 1, :], sp[:, 3, :], sp[:, 4, :], sp[:, 5, :], sp[:, 2, :]
                dve.wait_ge(cols_ready, 1)
                step(dve.tensor_scalar(q_, e, 2.0, None, ALU.add))
                step(dve.reciprocal(s2, q_))
                step(dve.tensor_tensor(s1, e, s2, ALU.mult))
                step(dve.tensor_tensor(s2, s1, s1, ALU.mult))
                step(dve.tensor_scalar(pw, s2, 1.0 / 17.0, None, ALU.mult))
                for k in (15, 13, 11, 9, 7, 5, 3):
                    step(dve.scalar_tensor_tensor(out=pw, in0=pw, scalar=1.0 / k, in1=s2, op0=ALU.add, op1=ALU.mult))
                step(dve.scalar_tensor_tensor(out=pw, in0=pw, scalar=1.0, in1=s1, op0=ALU.add, op1=ALU.mult))
                step(dve.tensor_scalar(q_, lam, -1.0, 0.0, ALU.mult, ALU.max))
                step(dve.scalar_tensor_tensor(out=pw, in0=pw, scalar=2.0, in1=q_, op0=ALU.mult, op1=ALU.add))
                step(dve.tensor_scalar(sp[:, 6, :], pw, 8.0, None, ALU.mult), wait=False)
                step(dve.tensor_scalar(sp[:, 7, :], pw, -8.0, None, ALU.mult))

            mean_square(0)
            for q in range(PIECES):
                norm_piece(0, q, xn_h)
            dve.wait_ge(c_ready, 1)
            for job, (mod, half) in enumerate(HEAD_JOBS):
                for u in range(UNITS):
                    n = job * UNITS + u
                    add_unit(n, u, head_acc[:, job, :], head_ring[:, n % HEAD_RING, :],
                             head_landed[n % HEAD_RING], 16 * (n // HEAD_RING + 1))
                    if n == 2 * UNITS:
                        parameters()
            for job, (mod, half) in enumerate(HEAD_JOBS):
                dve.wait_ge(job_summed, job + 1)
                col = mods[:, mod_at[mod], 8 * half:8 * half + 8]
                step(dve.tensor_tensor(col, ps[:, job, 0:8], bias_cols(mod, half), ALU.add))
                if mod == 1:
                    g = colA[:, A_NORM[0] + 8 * half:A_NORM[0] + 8 * half + 8]
                    step(dve.scalar_tensor_tensor(out=col, in0=col, scalar=1.0, in1=g, op0=ALU.add, op1=ALU.mult))
            for j in range(RING):
                split_lo(j, j)
            for q in range(PIECES + 1):
                if q < PIECES:
                    y_piece(0, q)
                if q:
                    y_low(0, q - 1)

            def ffn(f):
                g0, t0, l0 = G_FFN[f], T_FFN[f], L_FFN[f]
                if f == 0:
                    for j in range(RING, IN_SUBS):
                        split_lo(g0 + j, j)
                else:
                    behind_norm(g0, 1.0, 2)

                def product(g, count):
                    dve.wait_ge(silu_done, count)
                    dve.wait_ge(sub_multiplied, g)
                    dve.tensor_tensor(tm[:, :].rearrange("p (t n) -> p t n", t=TB), ps[:, 2:4, :],
                                      stage[:, :].rearrange("p (t n) -> p t n", t=TB), ALU.mult).then_inc(tm_written, 1)

                def pairs(lo, hi, job0):
                    with dve.Fori(lo, hi) as b:
                        g = g0 + IN_SUBS + b * (4 * IN_SUBS)
                        for j in range(4 * IN_SUBS):
                            split_lo(g + j, j)
                            half = j // (2 * IN_SUBS)
                            jj = j % (2 * IN_SUBS)
                            if jj == IN_SUBS + 2:
                                product(g + (2 * half + 1) * IN_SUBS, PAIRS * f + b * 2 + half + 1)
                            if jj == IN_SUBS + 4:
                                split_turned(hid_hi, hid_lo, b * 8 + 4 * half, l0 + 1 + half + b * 2)
                            if job0 is not None:
                                for u in units_after(j, 32):
                                    job_unit(b + job0, u)

                if f == 0:
                    pairs(0, LOOP_JOBS, 0)
                else:
                    pairs(0, 2, job0_of["ffn2"])
                    pairs(2, 5, None)
                g = g0 + IN_SUBS * (2 * PAIRS - 1)
                for j in range(IN_SUBS):
                    split_lo(g + j, j)
                g += IN_SUBS
                for i in range(N_OUT * OUT_SUBS):
                    n, j = divmod(i, OUT_SUBS)
                    split_lo(g + i, i)
                    if i == 2:
                        product(g, PAIRS * (f + 1))
                    if i == 4:
                        split_turned(hid_hi, hid_lo, 4 * (PAIRS - 1), l0 + PAIRS)
                    if j == 2 and n:
                        if n == 1:
                            dve.wait_ge(mods_made, 2 if f == 0 else len(JOBS))
                        add_resid(n - 1, g + n * OUT_SUBS, 0.5)
                    if f == 0 and i < 3 * 28:
                        for u in units_after(i % 28, 28):
                            job_unit(job0_of["ffn_out"] + i // 28, u)

            def behind_norm(g, half, stage_no):
                for j in range(RING - 1):
                    split_lo(g + j, j)
                add_resid(N_OUT - 1, g, half)
                mean_square(stage_no)
                dve.wait_ge(mods_made, (6, 10)[stage_no - 1])
                for q in range(3):
                    norm_piece(stage_no, q, xn)
                for q in range(PIECES + 1):
                    if q < PIECES:
                        y_piece(stage_no, q)
                    if q + 3 < PIECES:
                        norm_piece(stage_no, q + 3, xn)
                    if q:
                        y_low(stage_no, q - 1)
                    if q == 3:
                        split_lo(g + RING - 1, RING - 1)
                for j in range(RING, IN_SUBS):
                    split_lo(g + j, j)

            ffn(0)

            def conv(b0):
                dve.wait_ge(turn_kept, 1 + b0 // 4)
                for tap in range(TAPS - 1, -1, -1):
                    back = TAPS - 1 - tap
                    for b in range(b0, b0 + 4):
                        w = colB[:, B_TAP + tap * HEADS + b:B_TAP + tap * HEADS + b + 1]
                        if back == 0:
                            ins = dve.tensor_scalar(xc[:, b, :], xr_t[:, b, :], w, colB[:, B_CONVB + b:B_CONVB + b + 1],
                                                    ALU.mult, ALU.add)
                        else:
                            ins = dve.scalar_tensor_tensor(out=xc[:, b, back:S], in0=xr_t[:, b, 0:S - back], scalar=w,
                                                           in1=xc[:, b, back:S], op0=ALU.mult, op1=ALU.add)
                        if b == b0 + 3 and tap == 0:
                            ins.then_inc(conv_done, 1)
                        else:
                            step(ins, wait=(b == b0 + 3))

            def root_arg(b0):
                t, a, d = (v[:, b0:b0 + 4, :].rearrange("p b s -> p (b s)") for v in (lru_t, lru_r, xc))
                dve.wait_ge(decay_done, 2 * (b0 + 4))
                step(dve.tensor_tensor(d, a, a, ALU.mult))
                dve.scalar_tensor_tensor(out=t, in0=d, scalar=1.0, in1=t, op0=ALU.add, op1=ALU.mult).then_inc(root_in, 1)

            def recur(b):
                if b == 0:
                    dve.wait_ge(root_done, 1)
                step(dve.tensor_tensor(lru_i[:, b, :], lru_t[:, b, :], lru_i[:, b, :], ALU.mult))
                step(dve.tensor_tensor_scan(xc[:, b, :], lru_r[:, b, :], lru_i[:, b, :], 0.0, ALU.mult, ALU.add))
                dve.tensor_tensor(lru_t[:, b, :], xc[:, b, :], gr_t[:, b, :], ALU.mult).then_inc(ylru_ready, 1)

            def ylru_low(b0, count):
                dve.wait_ge(ylru_hi_done, count)
                dve.tensor_tensor(ylru_lo[:, b0:b0 + 4, :], lru_t[:, b0:b0 + 4, :],
                                  ylru_hi[:, b0:b0 + 4, :].bitcast(F32), ALU.subtract).then_inc(ylru_lo_done, 1)

            for ch in range(PROJ):
                for j in range(IN_SUBS):
                    i = ch * IN_SUBS + j
                    if i == 0:
                        behind_norm(G_MIX, 0.5, 1)
                    elif ch:
                        split_lo(G_MIX + i, i)
                    if j == 2 and 1 <= ch <= 8:
                        s = 2 * ((ch - 1) % 2)
                        dve.wait_ge(sub_multiplied, G_MIX + ch * IN_SUBS)
                        dve.tensor_copy(tm[:, :].rearrange("p (t n) -> p t n", t=TB), ps[:, s:s + 2, :]).then_inc(tm_written, 1)
                    if ch in (2, 3) and j == 6:
                        conv(4 * (ch - 2))
                    if ch == 6 and j == 0:
                        dve.wait_ge(gates_done, HEADS)
                        step(dve.tensor_tensor(lru_i[:, :, :], lru_i[:, :, :], xc[:, :, :], ALU.mult))
                    if ch == 7 and j in (1, 4):
                        root_arg(4 * (j // 4))
                    if ch in (8, 9) and j % 2 == 0:
                        recur(4 * (ch - 8) + j // 2)
                    if ch == 9 and j == 3:
                        ylru_low(0, 1)
                    for u in units_after((i - IN_SUBS) % 32, 32) if ch in range(1, 9) else ():
                        job_unit(job0_of["proj"] + (i - IN_SUBS) // 32, u)

            def gate_chunk(cc, g, first=False, b=None, half=0):
                for j in range(IN_SUBS):
                    split_lo(g + j, j)
                    if first:
                        if j == 0:
                            step(dve.memset(tm[:, 3 * P:3 * P + 1], 1.0))
                        if j == 3:
                            ylru_low(4, 2)
                        if j % 2:
                            job_unit(10, j // 2)
                    if b is not None and (half * IN_SUBS + j) % 4 == 3:
                        job_unit_at(10, b, 4 + (half * IN_SUBS + j) // 4)
                    if j == 4:
                        dve.wait_ge(betas, cc + 1)
                        dve.tensor_tensor_scan(tm[:, 0:3 * P][:, ::-1], stage[:, COLS:COLS + 3 * P][:, ::-1],
                                               unseen[:, :][:, ::-1], 1.0, ALU.mult, ALU.max).then_inc(scanned, 1)
                        dve.wait_ge(scanned, cc + 1)
                        dve.tensor_tensor(tm[:, COLS:COLS + 3 * P], stage[:, 0:3 * P], tm[:, 1:3 * P + 1],
                                          ALU.mult).then_inc(weights_ready, 1)
                dve.wait_ge(yat_hi_done, cc + 1)
                dve.tensor_tensor(yat_lo[:, bass.ds(cc, 1), :].rearrange("p a s -> p (a s)"), ps[:, 5, 0:S],
                                  yat_hi[:, bass.ds(cc, 1), :].rearrange("p a s -> p (a s)").bitcast(F32),
                                  ALU.subtract).then_inc(attn_split, 1)

            gate_chunk(0, G_GATES, first=True)
            with dve.Fori(0, (GATES - 2) // 2) as b:
                for half in range(2):
                    gate_chunk(b * 2 + 1 + half, G_GATES + IN_SUBS * (1 + half) + b * (2 * IN_SUBS), b=b, half=half)
            gate_chunk(GATES - 1, G_GATES + IN_SUBS * (GATES - 1))

            def merge_attn(n, g):
                dve.wait_ge(kept, 10)
                dve.wait_ge(sub_multiplied, g)
                dve.tensor_tensor(stage[:, :].rearrange("p (t n) -> p t n", t=TB), ps[:, 0:2, :],
                                  sg_merge[:, bass.ds(n, 1), :].rearrange("p a (t n) -> p (a t) n", t=TB),
                                  ALU.mult).then_inc(attn_merged, 1)

            def merge_lru(n, g):
                dve.wait_ge(sub_multiplied, g)
                dve.tensor_tensor(tm[:, :].rearrange("p (t n) -> p t n", t=TB), ps[:, 2:4, :],
                                  sg_merge[:, bass.ds(n + N_OUT, 1), :].rearrange("p a (t n) -> p (a t) n", t=TB),
                                  ALU.mult).then_inc(lru_merged, 1)
                dve.wait_ge(lru_merged, n + 1)
                dve.tensor_tensor(tm[:, :], tm[:, :], stage[:, :], ALU.add).then_inc(tm_written, 1)

            for i in range(BR_SUBS):
                split_lo(G_BR + i, i)
                for u in units_after(i, 32):
                    job_unit(11, u)
            for n in range(N_OUT - 1):
                g = G_BR + BR_SUBS + n * 2 * BR_SUBS
                for j in range(2 * BR_SUBS):
                    split_lo(g + j, j)
                    if j == 2:
                        merge_attn(n, g)
                    if j == 6:
                        merge_lru(n, g + BR_SUBS)
                    if j == 7:
                        split_turned(act_hi, act_lo, n * 4, L_BR + 1 + n)
                    for u in units_after(g + j - G_BR, 32):
                        job_unit(11, u)
            for j in range(BR_SUBS):
                split_lo(G_OUT - BR_SUBS + j, j)
                if j == 2:
                    merge_attn(N_OUT - 1, G_OUT - BR_SUBS)
            for i in range(N_OUT * IN_SUBS):
                n, j = divmod(i, IN_SUBS)
                split_lo(G_OUT + i, i)
                if i == 2:
                    merge_lru(N_OUT - 1, G_OUT)
                if i == 4:
                    split_turned(act_hi, act_lo, 4 * (N_OUT - 1), L_BR + N_OUT)
                if j == 2 and n:
                    if n == 1:
                        dve.wait_ge(mods_made, 12)
                    add_resid(n - 1, G_OUT + n * IN_SUBS, 1.0)
            ffn(1)
            add_resid(N_OUT - 1, G_FFN[1] + 2 * PAIRS * IN_SUBS + N_OUT * OUT_SUBS, 0.5)
            mean_square(3)
            dve.wait_ge(gain_landed, 16)
            for q in range(N_OUT):
                for t in range(TB):
                    r = resid[:, t, q * COLS:(q + 1) * COLS]
                    dve.scalar_tensor_tensor(out=r, in0=r, scalar=stat[:, 3, t:t + 1],
                                             in1=final_gain[:, q * COLS:(q + 1) * COLS],
                                             op0=ALU.mult, op1=ALU.mult).then_inc(out_ready, 1)

        @block.tensor
        def _(pe):
            def multiply(g, j, s, k, hi, lo, start, stop):
                pe.wait_ge(lo_split, g + 1)
                for q in range(2):
                    w_h = w_hi[:, j % RING, q * COLS:(q + 1) * COLS]
                    w_l = w_lo[:, j % RING, q * COLS:(q + 1) * COLS]
                    for t in range(TB):
                        x_h, x_l = (a[:, k + q, t * P:(t + 1) * P] for a in (hi, lo))
                        o = ps[:, s + t, :]
                        pe.matmul(o, x_h, w_h, start=(start and q == 0), stop=False)
                        pe.matmul(o, x_h, w_l, start=False, stop=False)
                        ins = pe.matmul(o, x_l, w_h, start=False, stop=(stop and q == 1))
                ins.then_inc(sub_multiplied, 1)

            def turn(src, bank, done, count=1):
                for k in range(4):
                    for t in range(TB):
                        at = k * S + t * P
                        ins = pe.transpose(ps[:, bank + at // COLS, at % COLS:at % COLS + P],
                                           src[:, t * COLS + k * P:t * COLS + (k + 1) * P], ident[:, :])
                ins.then_inc(done, count)

            def turn_xn(stage_no, src):
                for q in range(PIECES):
                    pe.wait_ge(xn_ready, PIECES * stage_no + q + 1)
                    for k in range(2):
                        for t in range(TB):
                            ins = pe.transpose(ps[:, q, k * S + t * P:k * S + (t + 1) * P],
                                               src[:, t, (2 * q + k) * P:(2 * q + k + 1) * P], ident[:, :])
                    ins.then_inc(xn_turned, 1)

            def first_chunk(g, stage_no, inner=None):
                for j in range(IN_SUBS):
                    pe.wait_ge(y_lo, PIECES * stage_no + j + 1)
                    multiply(g + j, j, 0, 2 * j, act_hi, act_lo, j == 0, j == IN_SUBS - 1)

            pe.wait_ge(consts_made, 2)
            turn_xn(0, xn_h)
            pe.wait_ge(x_kept, PIECES)
            pe.wait_ge(small_landed, 16 * SMALLS)
            pe.transpose(ps[:, 0, 0:112], rowsA, ident[0:112, 0:112])
            pe.transpose(ps[:, 0, 128:224], rowsB, ident[0:96, 0:96]).then_inc(rows_turned, 1)
            pe.wait_ge(consts_made, 7)
            pe.wait_ge(cols_ready, 1)
            for job in range(len(HEAD_JOBS)):
                pe.wait_ge(unit_added, (job + 1) * UNITS)
                for b in range(8):
                    ins = pe.matmul(ps[:, job, b:b + 1], head_acc[:, job, b * P:(b + 1) * P],
                                    ones[:, :], start=True, stop=True)
                ins.then_inc(job_summed, 1)

            def ffn(f):
                g0, t0, l0 = G_FFN[f], T_FFN[f], L_FFN[f]
                if f:
                    turn_xn(2, xn)
                first_chunk(g0, 2 * f)
                with pe.Fori(0, PAIRS - 1) as i:
                    g = g0 + IN_SUBS + i * (2 * IN_SUBS)
                    for j in range(IN_SUBS):
                        multiply(g + j, j, 2, 2 * j, act_hi, act_lo, j == 0, j == IN_SUBS - 1)
                    pe.wait_ge(silu_done, PAIRS * f + 1 + i)
                    for j in range(IN_SUBS):
                        multiply(g + IN_SUBS + j, j, 0, 2 * j, act_hi, act_lo, j == 0, j == IN_SUBS - 1)
                        if j == 1:
                            pe.wait_ge(tm_written, t0 + 1 + i)
                            turn(tm, 4, turned)
                g = g0 + IN_SUBS * (2 * PAIRS - 1)
                for j in range(IN_SUBS):
                    multiply(g + j, j, 2, 2 * j, act_hi, act_lo, j == 0, j == IN_SUBS - 1)
                g += IN_SUBS
                for i in range(N_OUT * OUT_SUBS):
                    n, j = divmod(i, OUT_SUBS)
                    if i == 0:
                        pe.wait_ge(silu_done, PAIRS * (f + 1))
                        pe.wait_ge(turn_lo, l0 + PAIRS - 1)
                    if j == 0 and n >= 2:
                        pe.wait_ge(resid_added, TB * (R_FFN[f] + n - 1))
                    if i == OUT_SUBS - 2:
                        pe.wait_ge(turn_lo, l0 + PAIRS)
                    multiply(g + i, i, 2 * (n % 2), 2 * j, hid_hi, hid_lo, j == 0, j == OUT_SUBS - 1)
                    if i == 1:
                        pe.wait_ge(tm_written, t0 + PAIRS)
                        turn(tm, 4, turned)

            ffn(0)

            turn_xn(1, xn)
            first_chunk(G_MIX, 1)
            for ch in range(1, PROJ):
                for j in range(IN_SUBS):
                    i = ch * IN_SUBS + j
                    multiply(G_MIX + i, i, 2 * (ch % 2), 2 * j, act_hi, act_lo, j == 0, j == IN_SUBS - 1)
                    if j == 1 and ch <= 8:
                        pe.wait_ge(tm_written, T_MIX + ch)
                        if ch > 1:
                            pe.wait_ge(turn_kept, ch - 1)
                        turn(tm, 4, turned)
                    if ch == 4:
                        if j == 0:
                            pe.wait_ge(lru_w_landed, 32)
                        if j in (0, 4):
                            pe.wait_ge(conv_done, 1 + j // 4)
                        if j >= 2:
                            pe.wait_ge(gates_done, j - 1)
                        pe.matmul(ps[:, 6 + j % 2, 0:S], w_gate_r[:, j, :], xc[:, j, :], start=True, stop=True)
                        pe.matmul(ps[:, 6 + j % 2, S:2 * S], w_gate_i[:, j, :], xc[:, j, :],
                                  start=True, stop=True).then_inc(gates_summed, 1)

            def gate_chunk(cc, g, s):
                pe.wait_ge(kept, cc + 1)
                for j in range(IN_SUBS):
                    multiply(g + j, j, s, 2 * j, act_hi, act_lo, j == 0, j == IN_SUBS - 1)
                    if j == 0:
                        pe.wait_ge(head_fetched, cc * 2 + 2)
                        z = ps[:, 6, 0:3 * P]
                        k_one = k_t[:, bass.ds(cc, 1), :].rearrange("p a s -> p (a s)")
                        pe.matmul(z, ident_bf[:, :], bar[:, :], start=True, stop=False)
                        pe.matmul(z[:, 0:P], q_one[:, 0:P], k_one[:, 0:P], start=False, stop=False)
                        pe.matmul(z[:, P:3 * P], q_one[:, P:2 * P], k_one, start=False, stop=True).then_inc(scores, 1)
                    if j == 3:
                        pe.wait_ge(weights_ready, cc + 1)
                        for b in range(3):
                            ins = pe.transpose(ps[:, 4, b * P:(b + 1) * P], tm[:, COLS + b * P:COLS + (b + 1) * P], ident[:, :])
                        ins.then_inc(weights_turned, 1)
                    if j == 5:
                        pe.wait_ge(weights_kept, cc + 1)
                        pe.matmul(ps[:, 5, 0:P], v_one[:, 0, :], w_turned[:, 0:P], start=True, stop=True)
                        pe.matmul(ps[:, 5, P:2 * P], v_one[:, 0, :], w_turned[:, P:2 * P], start=True, stop=False)
                        pe.matmul(ps[:, 5, P:2 * P], v_one[:, 1, :], w_turned[:, 2 * P:3 * P],
                                  start=False, stop=True).then_inc(head_out, 1)

            gate_chunk(0, G_GATES, 0)
            with pe.Fori(0, (GATES - 2) // 2) as b:
                for half in range(2):
                    gate_chunk(b * 2 + 1 + half, G_GATES + IN_SUBS * (1 + half) + b * (2 * IN_SUBS), 2 - 2 * half)
            gate_chunk(GATES - 1, G_GATES + IN_SUBS * (GATES - 1), 2)

            pe.wait_ge(kept, 9)
            pe.wait_ge(attn_split, HEADS)
            for j in range(BR_SUBS):
                multiply(G_BR + j, j, 0, 2 * j, yat_hi, yat_lo, j == 0, j == BR_SUBS - 1)
            with pe.Fori(0, N_OUT - 1) as n:
                g = G_BR + BR_SUBS + n * (2 * BR_SUBS)
                pe.wait_ge(kept, 10)
                for j in range(BR_SUBS):
                    multiply(g + j, j, 2, 2 * j, ylru_hi, ylru_lo, j == 0, j == BR_SUBS - 1)
                pe.wait_ge(attn_merged, n + 1)
                for j in range(BR_SUBS):
                    multiply(g + BR_SUBS + j, j, 0, 2 * j, yat_hi, yat_lo, j == 0, j == BR_SUBS - 1)
                    if j == 0:
                        pe.wait_ge(tm_written, T_BR + 1 + n)
                        turn(tm, 4, turned)
            for j in range(BR_SUBS):
                multiply(G_OUT - BR_SUBS + j, j, 2, 2 * j, ylru_hi, ylru_lo, j == 0, j == BR_SUBS - 1)
            for i in range(N_OUT * IN_SUBS):
                n, j = divmod(i, IN_SUBS)
                if i == 0:
                    pe.wait_ge(attn_merged, N_OUT)
                    pe.wait_ge(turn_lo, L_BR + N_OUT - 1)
                if j == 0 and n >= 2:
                    pe.wait_ge(resid_added, TB * (R_OUT + n - 1))
                if i == IN_SUBS - 2:
                    pe.wait_ge(turn_lo, L_BR + N_OUT)
                multiply(G_OUT + i, i, 2 * (n % 2), 2 * j, act_hi, act_lo, j == 0, j == IN_SUBS - 1)
                if i == 1:
                    pe.wait_ge(tm_written, T_BR + N_OUT)
                    turn(tm, 4, turned)
            ffn(1)


_INS = ["x", "c", "w_ada", "b_ada", "norm_ffn1", "w_ffn1_in", "w_ffn1_out", "norm_mix", "w_in",
        "conv_w", "conv_b", "w_rg_gate", "b_rg_gate", "w_in_gate", "b_in_gate", "lru_lambda",
        "w_branch_attn", "w_branch_lru", "w_out", "norm_ffn2", "w_ffn2_in", "w_ffn2_out", "norm_final"]


def kernel(**inputs):
    import numpy as _np
    import concourse.bacc as _bacc
    from concourse import mybir as _mybir
    from concourse.bass_utils import run_bass_kernel_spmd as _run

    nc = _bacc.Bacc("TRN2", target_bir_lowering=False, num_devices=1, dynamic_dma_scratch_size=1024)
    arrays, args = {}, []
    for name in _INS:
        a = _np.ascontiguousarray(inputs[name])
        arrays[f"in_{name}_dram"] = a
        args.append(nc.dram_tensor(f"in_{name}_dram", a.shape, _mybir.dt.from_np(a.dtype), kind="ExternalInput").ap())
    shape = _np.asarray(inputs["x"]).shape
    args.append(nc.dram_tensor("out_0_dram", shape, _mybir.dt.float32, kind="ExternalOutput").ap())
    macaron_layer(nc, *args)
    r = _run(nc, [arrays], core_ids=[0])
    return r.results[0]["out_0_dram"]
```

```python
from contextlib import ExitStack

import concourse.bass as bass
from concourse import mybir

ALU = mybir.AluOpType
ACT = mybir.ActivationFunctionType
AX = mybir.AxisListType
F32 = mybir.dt.float32
F32R = mybir.dt.float32r
BF16 = mybir.dt.bfloat16

P = 128
COLS = 512
RING = 4
JOB = 1024
MASKED = -1e30


def macaron_layer(nc, x, c, w_ada, b_ada, norm_ffn1, w_ffn1_in, w_ffn1_out, norm_mix, w_in,
                  conv_w, conv_b, w_rg_gate, b_rg_gate, w_in_gate, b_in_gate, lru_lambda,
                  w_branch_attn, w_branch_lru, w_out, norm_ffn2, w_ffn2_in, w_ffn2_out,
                  norm_final, out):
    D = x.shape[2]
    S = x.shape[1]
    TB = S // P
    KT = D // P
    FF = w_ffn1_out.shape[1]
    W = w_branch_attn.shape[1]
    HEADS = W // P
    TAPS = conv_w.shape[1]
    EPS = 1e-6
    SCALE = float(P) ** -0.5
    assert TB == 2 and KT == 16 and FF % COLS == 0 and HEADS == 8 and TAPS == 4

    IN_SUBS = KT // 2
    PAIRS = FF // COLS
    OUT_SUBS = FF // P // 2
    BR_SUBS = HEADS // 2
    N_OUT = D // COLS
    PROJ = 10
    GATES = 2 * N_OUT
    G_FFN = [0, 0]
    G_MIX = PAIRS * 2 * IN_SUBS + N_OUT * OUT_SUBS
    G_GATES = G_MIX + PROJ * IN_SUBS
    G_BR = G_GATES + GATES * IN_SUBS
    G_OUT = G_BR + N_OUT * 2 * BR_SUBS
    G_FFN[1] = G_OUT + N_OUT * IN_SUBS
    assert all(g % RING == 0 for g in (G_MIX, G_GATES, G_BR, G_OUT, G_FFN[1]))

    UNITS = KT
    JOBS = [(2, 0), (2, 1), (3, 0), (3, 1), (4, 0), (4, 1), (6, 0), (6, 1), (7, 0), (7, 1),
            (5, 0), (5, 1), (8, 0), (8, 1)]
    UNITS_BEFORE = N_OUT * UNITS
    HEAD_RING = 8
    LOOP_JOBS = (PAIRS - 3) // 2
    HEAD_CHUNKS = [(0, 6), (FF, 2), (COLS, 0)]
    HEAD_SUBS = 2 * len(HEAD_CHUNKS)
    LOAD_BEHIND = [[6, 8, 10, 12, 16, 18]] * (N_OUT - 1) + [[15, 15, 15, 15, 16, 16]]
    SPLIT_BEHIND = [[8, 10, 12, 14, 20, 22]] * (N_OUT - 1) + [[15, 15, 19, 19, 20, 20]]
    assert PAIRS % 2 == 1 and (HEAD_SUBS * N_OUT) % RING == 0

    def head_subs(behind, q, u):
        return [HEAD_SUBS * o + i for o in range(q + 1) if o < N_OUT
                for i, at in enumerate(behind[o]) if at == UNITS * (q - o) + u]

    def units_after(j, window):
        step = {32: 1.75, 24: 1.25}[window]
        return [u for u in range(UNITS) if int(u * step) == j]

    def job_col(job):
        mod, half = JOBS[job]
        return mod * D + half * JOB

    def subs(w):
        return w[0].rearrange("(s q p) n -> s p q n", q=2, p=P)

    v_ffn_in = [subs(w_ffn1_in), subs(w_ffn2_in)]
    v_ffn_out = [subs(w_ffn1_out), subs(w_ffn2_out)]
    v_in, v_attn, v_lru, v_out = subs(w_in), subs(w_branch_attn), subs(w_branch_lru), subs(w_out)
    v_ada = w_ada[0].rearrange("(p k) n -> p k n", k=UNITS)
    v_bada = b_ada.rearrange("a (m n) -> a m n", m=9)
    proj_col = [3 * W + COLS * i for i in range(4)] + [COLS * i for i in range(6)]
    gates_col = 5 * W

    ctx = ExitStack()
    with ctx:
        def sb(name, shape, dt=F32):
            return ctx.enter_context(nc.sbuf_tensor(name, shape, dt))

        def sem(name):
            return ctx.enter_context(nc.semaphore(name))

        resid = sb("resid", [P, TB, D])
        w_raw = sb("w_raw", [P, RING, 2 * COLS])
        w_hi = sb("w_hi", [P, RING, 2 * COLS], F32R)
        w_lo = sb("w_lo", [P, RING, 2 * COLS], F32R)
        ada_ring = sb("ada_ring", [P, 2, JOB])
        acc = sb("acc", [P, JOB])
        mod_row = sb("mod_row", [P, JOB])
        gate_row = sb("gate_row", [P, D])
        stage = sb("stage", [P, TB * COLS])
        tm = sb("tm", [P, TB * COLS])
        ident = sb("ident", [P, P])
        ident_bf = sb("ident_bf", [P, P], BF16)
        unseen = sb("unseen", [P, 3 * P], BF16)
        bar = sb("bar", [P, 3 * P], BF16)
        ones = sb("ones", [P, 1])
        spare = sb("spare", [P, 2])
        ccol = sb("ccol", [P, UNITS])
        colA = sb("colA", [P, 112])
        colB = sb("colB", [P, 96])
        mods = sb("mods", [P, 6, KT])
        ssq = sb("ssq", [P, TB, 4])
        stat = sb("stat", [P, 4, TB])
        sp = sb("sp", [P, 8, HEADS])
        rowsA, rowsB = mod_row[0:112, 0:P], mod_row[0:96, P:2 * P]
        GAIN, SHIFT = [0, 2, 4], [1, 3, 5]
        mod_at = {1: 0, 0: 1, 4: 2, 3: 3, 7: 4, 6: 5}

        def region(*tensors):
            with ExitStack() as r:
                return [r.enter_context(nc.sbuf_tensor(n, s, d)) for n, s, d in tensors]

        final_gain, = region(("final_gain", [P, D], F32))
        act_hi = sb("act_hi", [P, KT, S], F32R)
        act_lo = sb("act_lo", [P, KT, S], F32R)

        head_ring, head_acc, x_turned, xn_h = region(
            ("head_ring", [P, HEAD_RING, JOB], F32), ("head_acc", [P, 4, JOB], F32),
            ("x_turned", [P, KT, S], F32), ("xn_h", [P, TB, D], F32))
        xn, = region(("xn", [P, TB, D], F32))
        q_t, k_t, v_tok, ylru_hi, ylru_lo, sg_merge, xr_t, gr_t = region(
            ("q_t", [P, HEADS, S], F32), ("k_t", [P, HEADS, S], F32),
            ("v_tok", [P, TB, W], F32), ("ylru_hi", [P, HEADS, S], F32R),
            ("ylru_lo", [P, HEADS, S], F32R), ("sg_merge", [P, GATES, TB * COLS], F32),
            ("xr_t", [P, HEADS, S], F32), ("gr_t", [P, HEADS, S], F32))
        yat_hi, yat_lo, _, xc, lru_r, lru_i, lru_t, q_one, v_one, w_turned = region(
            ("yat_hi", [P, HEADS, S], F32R), ("yat_lo", [P, HEADS, S], F32R),
            ("gap", [P, 3, HEADS * S], F32), ("xc", [P, HEADS, S], F32),
            ("lru_r", [P, HEADS, S], F32), ("lru_i", [P, HEADS, S], F32),
            ("lru_t", [P, HEADS, S], F32), ("q_one", [P, S], F32),
            ("v_one", [P, TB, P], F32), ("w_turned", [P, 3 * P], F32))
        hid_hi = sb("hid_hi", [P, FF // P, S], F32R)
        hid_lo = sb("hid_lo", [P, FF // P, S], F32R)
        ps = ctx.enter_context(nc.psum_tensor("ps", [P, 8, COLS], F32))
        w_gate_r = gate_row[:, 0:HEADS * P].rearrange("p (n d) -> p n d", n=HEADS)
        w_gate_i = gate_row[:, HEADS * P:].rearrange("p (n d) -> p n d", n=HEADS)

        A_NORM = [0, 16, 32]
        A_BIAS = {1: 48, 0: 64, 4: 80, 3: 96}
        B_TAP, B_CONVB, B_BR, B_BI, B_LAM = 0, 32, 40, 48, 56
        B_BIAS = {7: 64, 6: 80}

        SMALLS = len(A_NORM) + len(A_BIAS) + 5 + len(B_BIAS)

        def bias_cols(mod, half):
            t, at = (colA, A_BIAS[mod]) if mod in A_BIAS else (colB, B_BIAS[mod])
            return t[:, at + 8 * half:at + 8 * half + 8]

        small_landed = sem("small_landed")
        c_landed = sem("c_landed")
        x_landed = [sem(f"x_landed{t}") for t in range(TB)]
        head_landed = [sem(f"head_landed{i}") for i in range(HEAD_RING)]
        w_landed = [sem(f"w_landed{i}") for i in range(RING)]
        ada_landed = [sem(f"ada_landed{i}") for i in range(2)]
        bias_landed = sem("bias_landed")
        lru_w_landed = sem("lru_w_landed")
        gain_landed = sem("gain_landed")
        stored = sem("stored")
        hi_rounded = sem("hi_rounded")
        lo_split = sem("lo_split")
        sub_multiplied = sem("sub_multiplied")
        unit_added = sem("unit_added")
        acc_free = sem("acc_free")
        mods_made = sem("mods_made")
        pool_step = sem("pool_step")
        consts_made = sem("consts_made")
        dve_step = sem("dve_step")
        c_ready = sem("c_ready")
        head_mods = sem("head_mods")
        rows_turned = sem("rows_turned")
        cols_ready = sem("cols_ready")
        job_summed = sem("job_summed")
        squared = sem("squared")
        ms_ready = sem("ms_ready")
        rstd_ready = sem("rstd_ready")
        xn_ready = sem("xn_ready")
        xn_turned = sem("xn_turned")
        x_kept = sem("x_kept")
        y_ready = sem("y_ready")
        y_hi = sem("y_hi")
        y_lo = sem("y_lo")
        silu_done = sem("silu_done")
        tm_written = sem("tm_written")
        turned = sem("turned")
        turn_hi = sem("turn_hi")
        turn_lo = sem("turn_lo")
        turn_kept = sem("turn_kept")
        resid_added = sem("resid_added")
        kept = sem("kept")
        conv_done = sem("conv_done")
        gates_summed = sem("gates_summed")
        gates_done = sem("gates_done")
        decay_done = sem("decay_done")
        root_in = sem("root_in")
        root_done = sem("root_done")
        ylru_ready = sem("ylru_ready")
        ylru_hi_done = sem("ylru_hi_done")
        ylru_lo_done = sem("ylru_lo_done")
        lam_abs = sem("lam_abs")
        lam_exp = sem("lam_exp")
        head_fetched = sem("head_fetched")
        scores = sem("scores")
        betas = sem("betas")
        scanned = sem("scanned")
        weights_ready = sem("weights_ready")
        weights_turned = sem("weights_turned")
        weights_kept = sem("weights_kept")
        head_out = sem("head_out")
        yat_hi_done = sem("yat_hi_done")
        attn_split = sem("attn_split")
        attn_merged = sem("attn_merged")
        lru_merged = sem("lru_merged")
        out_ready = sem("out_ready")

        T_FFN = [0, PAIRS + 8 + N_OUT]
        T_MIX = PAIRS
        T_BR = PAIRS + 8
        L_FFN = [0, PAIRS + N_OUT]
        L_BR = PAIRS
        R_FFN, R_OUT = [0, 2 * N_OUT], N_OUT
        job0_of = {"ffn_out": LOOP_JOBS, "proj": 8, "br": 11, "ffn2": 12}
        OUT_JOBS = 8 - LOOP_JOBS
        REST = (IN_SUBS + N_OUT * OUT_SUBS) // OUT_JOBS
        assert REST * OUT_JOBS == IN_SUBS + N_OUT * OUT_SUBS

        PIECES = IN_SUBS

        def y_space(q):
            return (stage, tm)[q // 2 % 2][:, (q % 2) * 2 * S:(q % 2 + 1) * 2 * S].rearrange("p (k s) -> p k s", s=S)

        def sqs(stage_no):
            return 8 * stage_no

        block = ctx.enter_context(nc.Block())

        @block.sync
        def _(sp_):
            def load_w(view, s, col, g, j, first=False):
                if not first:
                    sp_.wait_ge(lo_split, g - RING + 1)
                sp_.dma_start(w_raw[:, j % RING, :].rearrange("p (q n) -> p q n", q=2),
                              view[s, :, :, bass.ds(col, COLS)]).then_inc(w_landed[j % RING], 16)

            def load_unit(col, n, u, at=None):
                sp_.wait_ge(unit_added, n - 1)
                src = v_ada[:, u, bass.ds(col, JOB)] if at is None else \
                    v_ada[:, bass.ds(at, 1), bass.ds(col, JOB)].rearrange("p a n -> p (a n)")
                sp_.dma_start(ada_ring[:, u % 2, :], src).then_inc(ada_landed[u % 2], 16)

            def load_bias(job):
                mod, half = JOBS[job]
                sp_.dma_start(gate_row[0:1, half * JOB:(half + 1) * JOB],
                              v_bada[:, mod, half * JOB:(half + 1) * JOB]).then_inc(bias_landed, 16)

            sp_.dma_start(ccol[:, :], c[0].rearrange("(p k) -> p k", k=UNITS)).then_inc(c_landed, 16)
            x_v = x[0].rearrange("(t p) d -> t p d", p=P)
            for t in range(TB):
                sp_.dma_start(resid[:, t, :], x_v[t]).then_inc(x_landed[t], 16)
            smalls = [(rowsA[at:at + KT, :], src[0].rearrange("(k p) -> k p", p=P))
                      for at, src in zip(A_NORM, (norm_ffn1, norm_mix, norm_ffn2))]
            smalls += [(rowsA[at:at + KT, :], v_bada[0, mod, :].rearrange("(k p) -> k p", p=P))
                       for mod, at in A_BIAS.items()]
            smalls += [(rowsB[B_TAP:B_TAP + HEADS * TAPS, :], conv_w[0].rearrange("j (k p) -> (j k) p", p=P))]
            smalls += [(rowsB[at:at + HEADS, :], src[0].rearrange("(k p) -> k p", p=P))
                       for at, src in ((B_CONVB, conv_b), (B_BR, b_rg_gate), (B_BI, b_in_gate), (B_LAM, lru_lambda))]
            smalls += [(rowsB[at:at + KT, :], v_bada[0, mod, :].rearrange("(k p) -> k p", p=P))
                       for mod, at in B_BIAS.items()]
            assert len(smalls) == SMALLS
            def head_weights(q, u):
                for g in head_subs(LOAD_BEHIND, q, u):
                    o, i = divmod(g, HEAD_SUBS)
                    load_w(v_ffn_in[0], 2 * o + i % 2, HEAD_CHUNKS[i // 2][0], g, g, first=(g < RING))

            v_ada1 = w_ada[0].rearrange("(p k) (m d) -> p k m d", k=UNITS, m=9)
            for q in range(N_OUT):
                for u in range(UNITS):
                    n = q * UNITS + u
                    if n >= HEAD_RING:
                        sp_.wait_ge(unit_added, n - HEAD_RING + 1)
                    sp_.dma_start(head_ring[:, n % HEAD_RING, :].rearrange("p (m d) -> p m d", m=2),
                                  v_ada1[:, u, 0:2, q * COLS:(q + 1) * COLS]).then_inc(head_landed[n % HEAD_RING], 16)
                    for i in range(2 * n, min(2 * n + 2, SMALLS)):
                        sp_.dma_start(*smalls[i]).then_inc(small_landed, 16)
                    head_weights(q, u)
            for u in range(UNITS):
                head_weights(N_OUT, u)

            def ffn(f):
                g0 = G_FFN[f]
                if f == 0:
                    load_bias(0)
                    load_bias(1)
                else:
                    for j in range(IN_SUBS):
                        load_w(v_ffn_in[f], j, 0, g0 + j, j)
                    sp_.wait_ge(resid_added, TB * (R_OUT + N_OUT))
                    load_bias(12)
                    load_bias(13)

                    for j in range(2 * IN_SUBS):
                        load_w(v_ffn_in[f], j % IN_SUBS, (FF, COLS)[j // IN_SUBS], g0 + IN_SUBS + j, j)
                for j in range(2 * IN_SUBS):
                    load_w(v_ffn_in[f], j % IN_SUBS, (FF + COLS, 2 * COLS)[j // IN_SUBS],
                           g0 + 3 * IN_SUBS + j, j)

                def pairs(lo, hi, job0):
                    with sp_.Fori(lo, hi) as b:
                        for j in range(4 * IN_SUBS):
                            ch = j // IN_SUBS
                            col = b * (2 * COLS) + [FF + 2 * COLS, 3 * COLS, FF + 3 * COLS, 4 * COLS][ch]
                            load_w(v_ffn_in[f], j % IN_SUBS, col, g0 + 5 * IN_SUBS + b * (4 * IN_SUBS) + j, j)
                            if job0 is not None:
                                for u in units_after(j, 32):
                                    load_unit(b * JOB + job_col(job0), b * UNITS + UNITS_BEFORE + job0 * UNITS + u, u)

                if f == 0:
                    pairs(0, LOOP_JOBS, 0)
                else:
                    pairs(0, 2, job0_of["ffn2"])
                    pairs(2, LOOP_JOBS, None)
                g = g0 + IN_SUBS * (2 * PAIRS - 1)
                for i in range(IN_SUBS + N_OUT * OUT_SUBS):
                    if i < IN_SUBS:
                        load_w(v_ffn_in[f], i, FF + (PAIRS - 1) * COLS, g + i, i)
                    else:
                        n, j = divmod(i - IN_SUBS, OUT_SUBS)
                        load_w(v_ffn_out[f], j, n * COLS, g + i, i)
                    if f == 0:
                        job = job0_of["ffn_out"] + i // REST
                        for u in units_after(i % REST, REST):
                            load_unit(job_col(job), UNITS_BEFORE + job * UNITS + u, u)

            ffn(0)
            for ch in range(PROJ):
                for j in range(IN_SUBS):
                    i = ch * IN_SUBS + j
                    load_w(v_in, j, proj_col[ch], G_MIX + i, i)
                    if i == 2 * RING:
                        sp_.wait_ge(resid_added, TB * N_OUT)
                        for dst, src in ((w_gate_r, w_rg_gate), (w_gate_i, w_in_gate)):
                            sp_.dma_start(dst, src[0].rearrange("n c d -> c n d")).then_inc(lru_w_landed, 16)
                    for u in units_after((i - IN_SUBS) % 32, 32) if ch in range(1, 9) else ():
                        job = job0_of["proj"] + (i - IN_SUBS) // 32
                        load_unit(job_col(job), UNITS_BEFORE + job * UNITS + u, u)
            sp_.wait_ge(gates_done, HEADS)
            load_bias(10)
            load_bias(11)
            n10 = UNITS_BEFORE + 10 * UNITS
            for j in range(IN_SUBS):
                load_w(v_in, j, gates_col, G_GATES + j, j)
                if j % 2:
                    load_unit(job_col(10), n10 + j // 2, j // 2)
            with sp_.Fori(0, (GATES - 2) // 2) as b:
                for j in range(2 * IN_SUBS):
                    load_w(v_in, j % IN_SUBS, b * (2 * COLS) + gates_col + COLS * (1 + j // IN_SUBS),
                           G_GATES + IN_SUBS + b * (2 * IN_SUBS) + j, j)
                    if j % 4 == 3:
                        load_unit(job_col(10), b * 4 + (n10 + 4 + j // 4), j // 4, at=b * 4 + (4 + j // 4))
            for j in range(IN_SUBS):
                load_w(v_in, j, gates_col + COLS * (GATES - 1), G_GATES + IN_SUBS * (GATES - 1) + j, j)
            for i in range(N_OUT * 2 * BR_SUBS):
                n, j = divmod(i, 2 * BR_SUBS)
                load_w(v_attn if j < BR_SUBS else v_lru, j % BR_SUBS, n * COLS, G_BR + i, i)
                for u in units_after(i, 32):
                    load_unit(job_col(11), UNITS_BEFORE + 11 * UNITS + u, u)
            for i in range(N_OUT * IN_SUBS):
                n, j = divmod(i, IN_SUBS)
                load_w(v_out, j, n * COLS, G_OUT + i, i)
            ffn(1)
            sp_.wait_ge(sub_multiplied, G_FFN[1] + 2 * PAIRS * IN_SUBS)
            sp_.dma_start(final_gain[:, :], norm_final.rearrange("(a d) -> a d", a=1)
                          .to_broadcast([P, D])).then_inc(gain_landed, 16)
            out_v = out[0].rearrange("(t p) d -> p t d", p=P)
            for n in range(2 * N_OUT):
                t, q = n % TB, n // TB
                sp_.wait_ge(out_ready, n + 1)
                sp_.dma_start(out_v[:, t, q * COLS:(q + 1) * COLS],
                              resid[:, t, q * COLS:(q + 1) * COLS]).then_inc(stored, 16)
            sp_.wait_ge(stored, 16 * 2 * N_OUT)

        @block.gpsimd
        def _(pool):
            n_step = [0]

            def step(ins):
                n_step[0] += 1
                ins.then_inc(pool_step, 1)
                pool.wait_ge(pool_step, n_step[0])

            step(pool.memset(ident[:, :], 0.0))
            step(pool.memset(unseen[:, :], 0.0))
            step(pool.memset(bar[:, :], 0.0))
            pool.memset(ones[:, :], 1.0).then_inc(consts_made, 1)
            pool.affine_select(out=ident[:, :], in_=ident[:, :], compare_op=ALU.not_equal, fill=1.0,
                               base=0, pattern=[[-1, P]], channel_multiplier=1).then_inc(consts_made, 1)
            for m, fill in ((unseen, 1.0), (bar, MASKED)):
                for b in (0, 2):
                    pool.affine_select(out=m[:, b * P:(b + 1) * P], in_=m[:, b * P:(b + 1) * P],
                                       compare_op=ALU.is_gt, fill=fill, base=0, pattern=[[-1, P]],
                                       channel_multiplier=1).then_inc(consts_made, 1)
            pool.wait_ge(consts_made, 6)
            pool.tensor_copy(ident_bf[:, :], ident[:, :]).then_inc(consts_made, 1)
            pool.memset(spare[:, 0:1], 0.0).then_inc(acc_free, 1)

            def finish_job(job):
                mod, half = JOBS[job]
                pool.wait_ge(unit_added, UNITS_BEFORE + (job + 1) * UNITS)
                if job:
                    pool.wait_ge(mods_made, job)
                if mod in (2, 5, 8):
                    row = gate_row[:, half * JOB:(half + 1) * JOB]
                    pool.wait_ge(bias_landed, 16 * (2 if mod == 2 else 4 if mod == 5 else 6))
                    step(pool.tensor_tensor(acc[0:1, :], acc[0:1, :], row[0:1, :], ALU.add))
                    pool.partition_all_reduce(row, acc[:, :], P, bass.bass_isa.ReduceOp.add).then_inc(acc_free, 1)
                    pool.wait_ge(acc_free, job + 2)
                    pool.memset(spare[:, 0:1], 0.0).then_inc(mods_made, 1)
                    return
                pool.partition_all_reduce(mod_row[:, :], acc[:, :], P, bass.bass_isa.ReduceOp.add).then_inc(acc_free, 1)
                pool.wait_ge(acc_free, job + 2)
                blocks = mod_row[:, :].rearrange("p (b f) -> p b f", f=P)
                step(pool.tensor_tensor(blocks, blocks, ident[:, None, :].to_broadcast([P, 8, P]), ALU.mult))
                w = P // 2
                while w:
                    step(pool.tensor_tensor(blocks[:, :, 0:w], blocks[:, :, 0:w], blocks[:, :, w:2 * w], ALU.add))
                    w //= 2
                col = mods[:, mod_at[mod], 8 * half:8 * half + 8]
                if mod in (4, 7):
                    gain = A_NORM[1 if mod == 4 else 2] + 8 * half
                    step(pool.tensor_tensor(col, blocks[:, :, 0], bias_cols(mod, half), ALU.add))
                    step(pool.tensor_scalar(col, col, 1.0, None, ALU.add))
                    pool.tensor_tensor(col, col, colA[:, gain:gain + 8], ALU.mult).then_inc(mods_made, 1)
                else:
                    pool.tensor_tensor(col, blocks[:, :, 0], bias_cols(mod, half), ALU.add).then_inc(mods_made, 1)

            def fetch_head(h):
                pool.tensor_copy(q_one[:, :], q_t[:, bass.ds(h, 1), :].rearrange("p a s -> p (a s)")).then_inc(head_fetched, 1)
                pool.tensor_copy(v_one[:, :, :], v_tok[:, :, bass.ds(h * P, P)]).then_inc(head_fetched, 1)

            pool.wait_ge(cols_ready, 1)
            for job in range(10):
                finish_job(job)
            pool.wait_ge(turn_kept, 8)
            pool.wait_ge(kept, 2)
            pool.wait_ge(ylru_ready, HEADS)
            fetch_head(0)
            with pool.Fori(1, HEADS) as h:
                pool.wait_ge(head_out, h)
                fetch_head(h)
            for job in range(10, len(JOBS)):
                finish_job(job)

        @block.scalar
        def _(act):
            def round_hi(g, j, first=False):
                act.wait_ge(w_landed[j % RING], (g - j) * (16 // RING) + 16 * (j // RING + 1))
                if not first:
                    act.wait_ge(sub_multiplied, g - RING + 1)
                act.copy(w_hi[:, j % RING, :], w_raw[:, j % RING, :]).then_inc(hi_rounded, 1)

            def square(stage_no, i, t, n):
                if sqs(stage_no) + i:
                    act.wait_ge(squared, sqs(stage_no) + i)
                act.activation(tm[:, 0:COLS], resid[:, t, n * COLS:(n + 1) * COLS], ACT.Square,
                               accum_out=ssq[:, t, n:n + 1]).then_inc(squared, 1)

            def square_chunk(stage_no, n, r0):
                for t in range(TB):
                    act.wait_ge(resid_added, TB * (r0 + n) + t + 1)
                    square(stage_no, TB * n + t, t, n)

            def rstd(stage_no):
                act.wait_ge(ms_ready, stage_no + 1)
                act.activation(stat[:, 3, :], stat[:, 2, :], ACT.Sqrt).then_inc(rstd_ready, 1)

            def round_y(stage_no, q):
                act.wait_ge(y_ready, PIECES * stage_no + q + 1)
                act.copy(act_hi[:, 2 * q:2 * q + 2, :], y_space(q)).then_inc(y_hi, 1)

            def round_turned(dst, k, count):
                act.wait_ge(turned, count)
                act.copy(dst[:, bass.ds(k, 4), :], ps[:, 4:6, :].rearrange("p b (k s) -> p (b k) s", s=S)).then_inc(turn_hi, 1)

            act.wait_ge(c_landed, 16)
            act.activation(ccol[:, :], ccol[:, :], ACT.Silu).then_inc(c_ready, 1)
            for t in range(TB):
                act.wait_ge(x_landed[t], 16)
                for n in range(4):
                    square(0, 4 * t + n, t, n)
            rstd(0)
            act.wait_ge(rstd_ready, 1)
            for q in range(PIECES + 1):
                if q < PIECES:
                    for t in range(TB):
                        ins = act.activation(xn_h[:, t, 2 * q * P:2 * (q + 1) * P], resid[:, t, 2 * q * P:2 * (q + 1) * P],
                                             ACT.Copy, scale=stat[:, 3, t:t + 1])
                    ins.then_inc(xn_ready, 1)
                if q:
                    act.wait_ge(xn_turned, q)
                    act.copy(x_turned[:, 2 * q - 2:2 * q, :],
                             ps[:, q - 1, :].rearrange("p (k s) -> p k s", s=S)).then_inc(x_kept, 1)
                if q % 2:
                    round_hi(q // 2, q // 2, first=True)
            act.wait_ge(x_kept, PIECES)
            for o in range(N_OUT):
                if o == 1:
                    act.wait_ge(lam_abs, 1)
                    act.activation(sp[:, 1, :], sp[:, 0, :], ACT.Exp, scale=-1.0).then_inc(lam_exp, 1)
                before_y = 2 if o == N_OUT - 1 else RING
                for i in range(before_y if o else 0):
                    round_hi(HEAD_SUBS * o + i, HEAD_SUBS * o + i)
                act.wait_ge(head_mods, o + 1)
                for q in (2 * o, 2 * o + 1):
                    if q >= 4:
                        act.wait_ge(y_lo, q - 3)
                    for k in range(2):
                        at = 2 * q + k
                        ins = act.activation(y_space(q)[:, k, :], x_turned[:, at, :], ACT.Identity,
                                             scale=mods[:, GAIN[0], at:at + 1], bias=mods[:, SHIFT[0], at:at + 1])
                    ins.then_inc(y_ready, 1)
                    round_y(0, q)
                for i in range(before_y, HEAD_SUBS):
                    round_hi(HEAD_SUBS * o + i, HEAD_SUBS * o + i)

            def ffn(f):
                g0, t0 = G_FFN[f], T_FFN[f]

                def silu(g, bank=0):
                    act.wait_ge(sub_multiplied, g)
                    act.activation(stage[:, :], ps[:, bank:bank + 2, :], ACT.Silu).then_inc(silu_done, 1)

                def pair(i, carried=False):
                    g = g0 + IN_SUBS + i * (2 * IN_SUBS)
                    for j in range(IN_SUBS):
                        round_hi(g + j, j)
                        if j == 2:
                            if carried:
                                act.wait_ge(tm_written, 1)
                            silu(g)
                        if carried and j == 4:
                            round_turned(hid_hi, 0, 1)
                    for j in range(IN_SUBS, 2 * IN_SUBS):
                        round_hi(g + j, j)
                        if j == IN_SUBS + 4:
                            round_turned(hid_hi, i * 4, t0 + 1 + i)

                if f == 0:
                    silu(HEAD_SUBS * N_OUT - 4, bank=HEAD_CHUNKS[0][1])
                else:
                    behind_norm(g0, R_OUT, 2)
                    pair(0)
                pair(1, carried=(f == 0))
                with act.Fori(2, PAIRS - 1) as i:
                    pair(i)
                g = g0 + IN_SUBS * (2 * PAIRS - 1)
                for j in range(IN_SUBS):
                    round_hi(g + j, j)
                    if j == 2:
                        silu(g)
                g += IN_SUBS
                for i in range(N_OUT * OUT_SUBS):
                    n, j = divmod(i, OUT_SUBS)
                    round_hi(g + i, i)
                    if i == 4:
                        round_turned(hid_hi, 4 * (PAIRS - 1), t0 + PAIRS)
                    if j == 3 and n:
                        square_chunk(1 if f == 0 else 3, n - 1, R_FFN[f])

            def last_chunk(r0, stage_no):
                act.activation(spare[:, 1:2], stat[:, 3, 0:1], ACT.Sqrt)
                square_chunk(stage_no, N_OUT - 1, r0)
                rstd(stage_no)

            def behind_norm(g, r0, stage_no):
                for j in range(RING - 1):
                    round_hi(g + j, j)
                last_chunk(r0, stage_no)
                for q in range(3):
                    round_y(stage_no, q)
                round_hi(g + RING - 1, RING - 1)
                for q in range(3, PIECES):
                    round_y(stage_no, q)
                for j in range(RING, IN_SUBS):
                    round_hi(g + j, j)

            ffn(0)

            def lru_gate(b):
                act.wait_ge(gates_summed, b + 1)
                bank = ps[:, 6 + b % 2, :]
                act.activation(lru_r[:, b, :], bank[:, 0:S], ACT.Sigmoid, bias=colB[:, B_BR + b:B_BR + b + 1])
                act.activation(lru_i[:, b, :], bank[:, S:2 * S], ACT.Sigmoid,
                               bias=colB[:, B_BI + b:B_BI + b + 1]).then_inc(gates_done, 1)

            def lru_decay(b):
                if b == 0:
                    act.wait_ge(gates_done, HEADS)
                act.activation(lru_t[:, b, :], lru_r[:, b, :], ACT.Tanh, scale=sp[:, 6, b:b + 1]).then_inc(decay_done, 1)
                act.activation(lru_r[:, b, :], lru_r[:, b, :], ACT.Exp, scale=sp[:, 7, b:b + 1]).then_inc(decay_done, 1)

            for ch in range(PROJ):
                for j in range(IN_SUBS):
                    i = ch * IN_SUBS + j
                    if i == 0:
                        behind_norm(G_MIX, R_FFN[0], 1)
                    elif ch:
                        round_hi(G_MIX + i, i)
                    if ch == 9 and j == 2:
                        act.wait_ge(sub_multiplied, G_MIX + 9 * IN_SUBS)
                        act.copy(v_tok[:, :, 0:COLS], ps[:, 0:2, :]).then_inc(kept, 1)
                    if j == 4 and 1 <= ch <= 8:
                        d = (xr_t, gr_t, q_t, k_t)[(ch - 1) // 2][:, 4 * ((ch - 1) % 2):4 * ((ch - 1) % 2) + 4, :]
                        act.wait_ge(turned, T_MIX + ch)
                        act.activation(d, ps[:, 4:6, :].rearrange("p b (k s) -> p (b k) s", s=S),
                                       ACT.Gelu_apprx_tanh if ch in (3, 4) else ACT.Copy).then_inc(turn_kept, 1)
                    if ch == 4 and j >= RING:
                        lru_gate(j - RING)
                    if ch == 5 and j < RING:
                        lru_gate(j + RING)
                    if ch == 6:
                        lru_decay(j)
                    if ch == 7 and j == 7:
                        act.wait_ge(root_in, 2)
                        act.activation(lru_t[:, :, :], lru_t[:, :, :], ACT.Sqrt).then_inc(root_done, 1)
                    if ch == 9 and j == 1:
                        act.wait_ge(ylru_ready, 4)
                        act.copy(ylru_hi[:, 0:4, :], lru_t[:, 0:4, :]).then_inc(ylru_hi_done, 1)

            def gate_chunk(cc, g, s, first=False):
                for j in range(IN_SUBS):
                    round_hi(g + j, j)
                    if j == 0 and first:
                        act.wait_ge(ylru_ready, HEADS)
                        act.copy(ylru_hi[:, 4:8, :], lru_t[:, 4:8, :]).then_inc(ylru_hi_done, 1)
                    if j == 2:
                        act.wait_ge(sub_multiplied, g)
                        if first:
                            act.copy(v_tok[:, :, COLS:2 * COLS], ps[:, 2:4, :]).then_inc(kept, 1)
                        else:
                            keep_gate(cc - 1, s)
                    if j == 3:
                        act.wait_ge(scores, cc + 1)
                        z = ps[:, 6, 0:3 * P]
                        act.activation(stage[:, 0:3 * P], z, ACT.Sigmoid, scale=SCALE)
                        act.activation(stage[:, COLS:COLS + 3 * P], z, ACT.Sigmoid, scale=-SCALE).then_inc(betas, 1)
                act.wait_ge(weights_turned, cc + 1)
                act.copy(w_turned[:, :], ps[:, 4, 0:3 * P]).then_inc(weights_kept, 1)
                act.wait_ge(head_out, cc + 1)
                act.copy(yat_hi[:, bass.ds(cc, 1), :].rearrange("p a s -> p (a s)"), ps[:, 5, 0:S]).then_inc(yat_hi_done, 1)

            def keep_gate(cc, s):
                act.activation(sg_merge[:, bass.ds(cc, 1), :].rearrange("p a n -> p (a n)"),
                               ps[:, s:s + 2, :], ACT.Sigmoid).then_inc(kept, 1)

            gate_chunk(0, G_GATES, 2, first=True)
            act.wait_ge(ylru_lo_done, 2)
            with act.Fori(0, (GATES - 2) // 2) as b:
                for half in range(2):
                    gate_chunk(b * 2 + 1 + half, G_GATES + IN_SUBS * (1 + half) + b * (2 * IN_SUBS), 2 * half)
            gate_chunk(GATES - 1, G_GATES + IN_SUBS * (GATES - 1), 0)

            for j in range(BR_SUBS):
                round_hi(G_BR + j, j)
                if j == 2:
                    act.wait_ge(sub_multiplied, G_BR)
                    keep_gate(GATES - 1, 2)
            with act.Fori(0, N_OUT - 1) as n:
                g = G_BR + BR_SUBS + n * (2 * BR_SUBS)
                for j in range(2 * BR_SUBS):
                    round_hi(g + j, j)
                round_turned(act_hi, n * 4, T_BR + 1 + n)
            for j in range(BR_SUBS):
                round_hi(G_OUT - BR_SUBS + j, j)
            for i in range(N_OUT * IN_SUBS):
                n, j = divmod(i, IN_SUBS)
                round_hi(G_OUT + i, i)
                if i == 4:
                    round_turned(act_hi, 4 * (N_OUT - 1), T_BR + N_OUT)
                if j == 3 and n:
                    square_chunk(2, n - 1, R_OUT)
            ffn(1)
            last_chunk(R_FFN[1], 3)

        @block.vector
        def _(dve):
            n_step = [0]

            def step(ins, wait=True):
                n_step[0] += 1
                ins.then_inc(dve_step, 1)
                if wait:
                    dve.wait_ge(dve_step, n_step[0])

            def split_lo(g, j):
                dve.wait_ge(hi_rounded, g + 1)
                dve.tensor_tensor(w_lo[:, j % RING, :], w_raw[:, j % RING, :],
                                  w_hi[:, j % RING, :].bitcast(F32), ALU.subtract).then_inc(lo_split, 1)

            def add_unit(n, u, dst, src, landed, count, jobs_before=None):
                dve.wait_ge(landed, count)
                if u == 0:
                    if jobs_before is not None:
                        dve.wait_ge(acc_free, jobs_before + 1)
                    dve.tensor_scalar(dst, src, ccol[:, 0:1], None, ALU.mult).then_inc(unit_added, 1)
                else:
                    dve.wait_ge(unit_added, n)
                    dve.scalar_tensor_tensor(out=dst, in0=src, scalar=ccol[:, u:u + 1], in1=dst,
                                             op0=ALU.mult, op1=ALU.add).then_inc(unit_added, 1)

            def job_unit(job, u):
                add_unit(job * UNITS + (UNITS_BEFORE + u), u, acc[:, :], ada_ring[:, u % 2, :],
                         ada_landed[u % 2], job * (16 * UNITS // 2) + 16 * (u // 2 + 1), jobs_before=job)

            def job_unit_at(job, b, u):
                dve.wait_ge(ada_landed[u % 2], b * 32 + 16 * (job * UNITS // 2 + u // 2 + 1))
                dve.wait_ge(unit_added, b * 4 + (UNITS_BEFORE + job * UNITS + u))
                dve.scalar_tensor_tensor(out=acc[:, :], in0=ada_ring[:, u % 2, :], scalar=ccol[:, bass.ds(b * 4 + u, 1)],
                                         in1=acc[:, :], op0=ALU.mult, op1=ALU.add).then_inc(unit_added, 1)

            def mean_square(stage_no):
                dve.wait_ge(squared, sqs(stage_no + 1))
                step(dve.tensor_reduce(stat[:, 0, :], ssq[:, :, :], AX.X, ALU.add))
                step(dve.tensor_scalar(stat[:, 1, :], stat[:, 0, :], 1.0 / D, EPS, ALU.mult, ALU.add))
                dve.reciprocal(stat[:, 2, :], stat[:, 1, :]).then_inc(ms_ready, 1)

            def norm_piece(stage_no, q):
                cols = slice(q * 2 * P, (q + 1) * 2 * P)
                for t in range(TB):
                    ins = dve.tensor_scalar(xn[:, t, cols], resid[:, t, cols], stat[:, 3, t:t + 1], None, ALU.mult)
                ins.then_inc(xn_ready, 1)

            def y_piece(stage_no, q):
                if q >= 4:
                    dve.wait_ge(y_lo, PIECES * stage_no + q - 3)
                src = ps[:, q, :].rearrange("p (k s) -> p k s", s=S)
                dve.wait_ge(xn_turned, PIECES * stage_no + q + 1)
                for k in range(2):
                    ins = dve.tensor_scalar(y_space(q)[:, k, :], src[:, k, :],
                                            mods[:, GAIN[stage_no], 2 * q + k:2 * q + k + 1],
                                            mods[:, SHIFT[stage_no], 2 * q + k:2 * q + k + 1], ALU.mult, ALU.add)
                ins.then_inc(y_ready, 1)

            def y_low(stage_no, q):
                dve.wait_ge(y_hi, PIECES * stage_no + q + 1)
                dve.tensor_tensor(act_lo[:, 2 * q:2 * q + 2, :], y_space(q),
                                  act_hi[:, 2 * q:2 * q + 2, :].bitcast(F32), ALU.subtract).then_inc(y_lo, 1)

            def split_turned(hi, lo, k, count):
                dve.wait_ge(turn_hi, count)
                dve.tensor_tensor(lo[:, bass.ds(k, 4), :], ps[:, 4:6, :].rearrange("p b (k s) -> p (b k) s", s=S),
                                  hi[:, bass.ds(k, 4), :].bitcast(F32), ALU.subtract).then_inc(turn_lo, 1)

            def add_resid(n, g_end, half):
                dve.wait_ge(sub_multiplied, g_end)
                for t in range(TB):
                    prod = stage[:, t * COLS:(t + 1) * COLS]
                    r = resid[:, t, n * COLS:(n + 1) * COLS]
                    step(dve.scalar_tensor_tensor(out=prod, in0=ps[:, 2 * (n % 2) + t, :], scalar=half,
                                                  in1=gate_row[:, n * COLS:(n + 1) * COLS],
                                                  op0=ALU.mult, op1=ALU.mult))
                    dve.tensor_tensor(r, r, prod, ALU.add).then_inc(resid_added, 1)

            def columns():
                dve.wait_ge(rows_turned, 1)
                step(dve.tensor_copy(colA[:, :], ps[:, 0, 0:112]), wait=False)
                step(dve.tensor_copy(colB[:, :], ps[:, 0, 128:224]))
                dve.memset(sp[:, 2, :], 0.0).then_inc(cols_ready, 1)
                lam = colB[:, B_LAM:B_LAM + HEADS]
                dve.scalar_tensor_tensor(out=sp[:, 0, :], in0=lam, scalar=-1.0, in1=lam,
                                         op0=ALU.mult, op1=ALU.max).then_inc(lam_abs, 1)

            def decay_rates():
                lam = colB[:, B_LAM:B_LAM + HEADS]
                dve.wait_ge(lam_exp, 1)
                e, s1, s2, pw, q_ = sp[:, 1, :], sp[:, 3, :], sp[:, 4, :], sp[:, 5, :], sp[:, 2, :]
                dve.wait_ge(cols_ready, 1)
                step(dve.tensor_scalar(q_, e, 2.0, None, ALU.add))
                step(dve.reciprocal(s2, q_))
                step(dve.tensor_tensor(s1, e, s2, ALU.mult))
                step(dve.tensor_tensor(s2, s1, s1, ALU.mult))
                step(dve.tensor_scalar(pw, s2, 1.0 / 17.0, None, ALU.mult))
                for k in (15, 13, 11, 9, 7, 5, 3):
                    step(dve.scalar_tensor_tensor(out=pw, in0=pw, scalar=1.0 / k, in1=s2, op0=ALU.add, op1=ALU.mult))
                step(dve.scalar_tensor_tensor(out=pw, in0=pw, scalar=1.0, in1=s1, op0=ALU.add, op1=ALU.mult))
                step(dve.tensor_scalar(q_, lam, -1.0, 0.0, ALU.mult, ALU.max))
                step(dve.scalar_tensor_tensor(out=pw, in0=pw, scalar=2.0, in1=q_, op0=ALU.mult, op1=ALU.add))
                step(dve.tensor_scalar(sp[:, 6, :], pw, 8.0, None, ALU.mult), wait=False)
                step(dve.tensor_scalar(sp[:, 7, :], pw, -8.0, None, ALU.mult))

            def head_cols(o):
                dve.wait_ge(job_summed, o + 1)
                shift, gain = (mods[:, m, 4 * o:4 * o + 4] for m in (SHIFT[0], GAIN[0]))
                bias = {mod: bias_cols(mod, o // 2)[:, 4 * (o % 2):4 * (o % 2) + 4] for mod in (0, 1)}
                step(dve.tensor_tensor(gain, ps[:, 4, 8 * o + 4:8 * o + 8], bias[1], ALU.add), wait=False)
                step(dve.tensor_tensor(shift, ps[:, 4, 8 * o:8 * o + 4], bias[0], ALU.add))
                dve.scalar_tensor_tensor(out=gain, in0=gain, scalar=1.0, in1=colA[:, A_NORM[0] + 4 * o:A_NORM[0] + 4 * o + 4],
                                         op0=ALU.add, op1=ALU.mult).then_inc(head_mods, 1)

            def behind_unit(q, u):
                n = q * UNITS + u
                if n == 3:
                    mean_square(0)
                if n == UNITS - 2:
                    columns()
                if n == 2 * UNITS:
                    decay_rates()
                if q and u == 0:
                    head_cols(q - 1)
                if q and u in (2, 3):
                    y_low(0, 2 * (q - 1) + u - 2)
                for g in head_subs(SPLIT_BEHIND, q, u):
                    split_lo(g, g)

            dve.wait_ge(c_ready, 1)
            for q in range(N_OUT):
                for u in range(UNITS):
                    n = q * UNITS + u
                    add_unit(n, u, head_acc[:, q, :], head_ring[:, n % HEAD_RING, :],
                             head_landed[n % HEAD_RING], 16 * (n // HEAD_RING + 1))
                    behind_unit(q, u)
            for u in range(UNITS):
                behind_unit(N_OUT, u)

            def ffn(f):
                g0, t0, l0 = G_FFN[f], T_FFN[f], L_FFN[f]

                def product(g, count):
                    dve.wait_ge(silu_done, count)
                    dve.wait_ge(sub_multiplied, g)
                    dve.tensor_tensor(tm[:, :].rearrange("p (t n) -> p t n", t=TB), ps[:, 2:4, :],
                                      stage[:, :].rearrange("p (t n) -> p t n", t=TB), ALU.mult).then_inc(tm_written, 1)

                def pair(i, j, carried=False):
                    g = g0 + IN_SUBS + i * (2 * IN_SUBS)
                    split_lo(g + j, j)
                    if carried and j == 1:
                        product(HEAD_SUBS * N_OUT - 2, 1)
                    if carried and j == 5:
                        split_turned(hid_hi, hid_lo, 0, 1)
                    if j == IN_SUBS + 2:
                        product(g + IN_SUBS, PAIRS * f + 1 + i)
                    if j == IN_SUBS + 4:
                        split_turned(hid_hi, hid_lo, i * 4, l0 + 1 + i)

                def pairs(lo, hi, job0):
                    with dve.Fori(lo, hi) as b:
                        for j in range(4 * IN_SUBS):
                            pair(b * 2 + (2 + j // (2 * IN_SUBS)), j % (2 * IN_SUBS))
                            if job0 is not None:
                                for u in units_after(j, 32):
                                    job_unit(b + job0, u)

                if f:
                    behind_norm(g0, 1.0, 2)
                    for j in range(2 * IN_SUBS):
                        pair(0, j)
                for j in range(2 * IN_SUBS):
                    pair(1, j, carried=(f == 0))
                if f == 0:
                    pairs(0, LOOP_JOBS, 0)
                else:
                    pairs(0, 2, job0_of["ffn2"])
                    pairs(2, LOOP_JOBS, None)

                def rest_units(i):
                    if f == 0:
                        for u in units_after(i % REST, REST):
                            job_unit(job0_of["ffn_out"] + i // REST, u)

                g = g0 + IN_SUBS * (2 * PAIRS - 1)
                for j in range(IN_SUBS):
                    split_lo(g + j, j)
                    rest_units(j)
                g += IN_SUBS
                for i in range(N_OUT * OUT_SUBS):
                    n, j = divmod(i, OUT_SUBS)
                    split_lo(g + i, i)
                    if i == 2:
                        product(g, PAIRS * (f + 1))
                    if i == 4:
                        split_turned(hid_hi, hid_lo, 4 * (PAIRS - 1), l0 + PAIRS)
                    if j == 2 and n:
                        if n == 1:
                            dve.wait_ge(mods_made, 2 if f == 0 else len(JOBS))
                        add_resid(n - 1, g + n * OUT_SUBS, 0.5)
                    rest_units(IN_SUBS + i)

            def behind_norm(g, half, stage_no):
                for j in range(RING - 1):
                    split_lo(g + j, j)
                add_resid(N_OUT - 1, g, half)
                mean_square(stage_no)
                dve.wait_ge(rstd_ready, stage_no + 1)
                dve.wait_ge(mods_made, (6, 10)[stage_no - 1])
                for q in range(3):
                    norm_piece(stage_no, q)
                for q in range(PIECES + 1):
                    if q < PIECES:
                        y_piece(stage_no, q)
                    if q + 3 < PIECES:
                        norm_piece(stage_no, q + 3)
                    if q:
                        y_low(stage_no, q - 1)
                    if q == 3:
                        split_lo(g + RING - 1, RING - 1)
                for j in range(RING, IN_SUBS):
                    split_lo(g + j, j)

            ffn(0)

            def conv(b0):
                dve.wait_ge(turn_kept, 1 + b0 // 4)
                for tap in range(TAPS - 1, -1, -1):
                    back = TAPS - 1 - tap
                    for b in range(b0, b0 + 4):
                        w = colB[:, B_TAP + tap * HEADS + b:B_TAP + tap * HEADS + b + 1]
                        if back == 0:
                            ins = dve.tensor_scalar(xc[:, b, :], xr_t[:, b, :], w, colB[:, B_CONVB + b:B_CONVB + b + 1],
                                                    ALU.mult, ALU.add)
                        else:
                            ins = dve.scalar_tensor_tensor(out=xc[:, b, back:S], in0=xr_t[:, b, 0:S - back], scalar=w,
                                                           in1=xc[:, b, back:S], op0=ALU.mult, op1=ALU.add)
                        if b == b0 + 3 and tap == 0:
                            ins.then_inc(conv_done, 1)
                        else:
                            step(ins, wait=(b == b0 + 3))

            def root_arg(b0):
                t, a, d = (v[:, b0:b0 + 4, :].rearrange("p b s -> p (b s)") for v in (lru_t, lru_r, xc))
                dve.wait_ge(decay_done, 2 * (b0 + 4))
                step(dve.tensor_tensor(d, a, a, ALU.mult))
                dve.scalar_tensor_tensor(out=t, in0=d, scalar=1.0, in1=t, op0=ALU.add, op1=ALU.mult).then_inc(root_in, 1)

            def recur(b):
                if b == 0:
                    dve.wait_ge(root_done, 1)
                step(dve.tensor_tensor(lru_i[:, b, :], lru_t[:, b, :], lru_i[:, b, :], ALU.mult))
                step(dve.tensor_tensor_scan(xc[:, b, :], lru_r[:, b, :], lru_i[:, b, :], 0.0, ALU.mult, ALU.add))
                dve.tensor_tensor(lru_t[:, b, :], xc[:, b, :], gr_t[:, b, :], ALU.mult).then_inc(ylru_ready, 1)

            def ylru_low(b0, count):
                dve.wait_ge(ylru_hi_done, count)
                dve.tensor_tensor(ylru_lo[:, b0:b0 + 4, :], lru_t[:, b0:b0 + 4, :],
                                  ylru_hi[:, b0:b0 + 4, :].bitcast(F32), ALU.subtract).then_inc(ylru_lo_done, 1)

            for ch in range(PROJ):
                for j in range(IN_SUBS):
                    i = ch * IN_SUBS + j
                    if i == 0:
                        behind_norm(G_MIX, 0.5, 1)
                    elif ch:
                        split_lo(G_MIX + i, i)
                    if j == 2 and 1 <= ch <= 8:
                        s = 2 * ((ch - 1) % 2)
                        dve.wait_ge(sub_multiplied, G_MIX + ch * IN_SUBS)
                        dve.tensor_copy(tm[:, :].rearrange("p (t n) -> p t n", t=TB), ps[:, s:s + 2, :]).then_inc(tm_written, 1)
                    if ch in (2, 3) and j == 6:
                        conv(4 * (ch - 2))
                    if ch == 6 and j == 0:
                        dve.wait_ge(gates_done, HEADS)
                        step(dve.tensor_tensor(lru_i[:, :, :], lru_i[:, :, :], xc[:, :, :], ALU.mult))
                    if ch == 7 and j in (1, 4):
                        root_arg(4 * (j // 4))
                    if ch in (8, 9) and j % 2 == 0:
                        recur(4 * (ch - 8) + j // 2)
                    if ch == 9 and j == 3:
                        ylru_low(0, 1)
                    for u in units_after((i - IN_SUBS) % 32, 32) if ch in range(1, 9) else ():
                        job_unit(job0_of["proj"] + (i - IN_SUBS) // 32, u)

            def gate_chunk(cc, g, first=False, b=None, half=0):
                for j in range(IN_SUBS):
                    split_lo(g + j, j)
                    if first:
                        if j == 0:
                            step(dve.memset(tm[:, 3 * P:3 * P + 1], 1.0))
                        if j == 3:
                            ylru_low(4, 2)
                        if j % 2:
                            job_unit(10, j // 2)
                    if b is not None and (half * IN_SUBS + j) % 4 == 3:
                        job_unit_at(10, b, 4 + (half * IN_SUBS + j) // 4)
                    if j == 4:
                        dve.wait_ge(betas, cc + 1)
                        dve.tensor_tensor_scan(tm[:, 0:3 * P][:, ::-1], stage[:, COLS:COLS + 3 * P][:, ::-1],
                                               unseen[:, :][:, ::-1], 1.0, ALU.mult, ALU.max).then_inc(scanned, 1)
                        dve.wait_ge(scanned, cc + 1)
                        dve.tensor_tensor(tm[:, COLS:COLS + 3 * P], stage[:, 0:3 * P], tm[:, 1:3 * P + 1],
                                          ALU.mult).then_inc(weights_ready, 1)
                dve.wait_ge(yat_hi_done, cc + 1)
                dve.tensor_tensor(yat_lo[:, bass.ds(cc, 1), :].rearrange("p a s -> p (a s)"), ps[:, 5, 0:S],
                                  yat_hi[:, bass.ds(cc, 1), :].rearrange("p a s -> p (a s)").bitcast(F32),
                                  ALU.subtract).then_inc(attn_split, 1)

            gate_chunk(0, G_GATES, first=True)
            with dve.Fori(0, (GATES - 2) // 2) as b:
                for half in range(2):
                    gate_chunk(b * 2 + 1 + half, G_GATES + IN_SUBS * (1 + half) + b * (2 * IN_SUBS), b=b, half=half)
            gate_chunk(GATES - 1, G_GATES + IN_SUBS * (GATES - 1))

            def merge_attn(n, g):
                dve.wait_ge(kept, 10)
                dve.wait_ge(sub_multiplied, g)
                dve.tensor_tensor(stage[:, :].rearrange("p (t n) -> p t n", t=TB), ps[:, 0:2, :],
                                  sg_merge[:, bass.ds(n, 1), :].rearrange("p a (t n) -> p (a t) n", t=TB),
                                  ALU.mult).then_inc(attn_merged, 1)

            def merge_lru(n, g):
                dve.wait_ge(sub_multiplied, g)
                dve.tensor_tensor(tm[:, :].rearrange("p (t n) -> p t n", t=TB), ps[:, 2:4, :],
                                  sg_merge[:, bass.ds(n + N_OUT, 1), :].rearrange("p a (t n) -> p (a t) n", t=TB),
                                  ALU.mult).then_inc(lru_merged, 1)
                dve.wait_ge(lru_merged, n + 1)
                dve.tensor_tensor(tm[:, :], tm[:, :], stage[:, :], ALU.add).then_inc(tm_written, 1)

            for i in range(BR_SUBS):
                split_lo(G_BR + i, i)
                for u in units_after(i, 32):
                    job_unit(11, u)
            for n in range(N_OUT - 1):
                g = G_BR + BR_SUBS + n * 2 * BR_SUBS
                for j in range(2 * BR_SUBS):
                    split_lo(g + j, j)
                    if j == 2:
                        merge_attn(n, g)
                    if j == 6:
                        merge_lru(n, g + BR_SUBS)
                    if j == 7:
                        split_turned(act_hi, act_lo, n * 4, L_BR + 1 + n)
                    for u in units_after(g + j - G_BR, 32):
                        job_unit(11, u)
            for j in range(BR_SUBS):
                split_lo(G_OUT - BR_SUBS + j, j)
                if j == 2:
                    merge_attn(N_OUT - 1, G_OUT - BR_SUBS)
            for i in range(N_OUT * IN_SUBS):
                n, j = divmod(i, IN_SUBS)
                split_lo(G_OUT + i, i)
                if i == 2:
                    merge_lru(N_OUT - 1, G_OUT)
                if i == 4:
                    split_turned(act_hi, act_lo, 4 * (N_OUT - 1), L_BR + N_OUT)
                if j == 2 and n:
                    if n == 1:
                        dve.wait_ge(mods_made, 12)
                    add_resid(n - 1, G_OUT + n * IN_SUBS, 1.0)
            ffn(1)
            add_resid(N_OUT - 1, G_FFN[1] + 2 * PAIRS * IN_SUBS + N_OUT * OUT_SUBS, 0.5)
            mean_square(3)
            dve.wait_ge(rstd_ready, 4)
            dve.wait_ge(gain_landed, 16)
            for q in range(N_OUT):
                for t in range(TB):
                    r = resid[:, t, q * COLS:(q + 1) * COLS]
                    dve.scalar_tensor_tensor(out=r, in0=r, scalar=stat[:, 3, t:t + 1],
                                             in1=final_gain[:, q * COLS:(q + 1) * COLS],
                                             op0=ALU.mult, op1=ALU.mult).then_inc(out_ready, 1)

        @block.tensor
        def _(pe):
            def multiply(g, j, s, k, hi, lo, start, stop):
                pe.wait_ge(lo_split, g + 1)
                for q in range(2):
                    w_h = w_hi[:, j % RING, q * COLS:(q + 1) * COLS]
                    w_l = w_lo[:, j % RING, q * COLS:(q + 1) * COLS]
                    for t in range(TB):
                        x_h, x_l = (a[:, k + q, t * P:(t + 1) * P] for a in (hi, lo))
                        o = ps[:, s + t, :]
                        pe.matmul(o, x_h, w_h, start=(start and q == 0), stop=False)
                        pe.matmul(o, x_h, w_l, start=False, stop=False)
                        ins = pe.matmul(o, x_l, w_h, start=False, stop=(stop and q == 1))
                ins.then_inc(sub_multiplied, 1)

            def turn(src, bank, done, count=1):
                for k in range(4):
                    for t in range(TB):
                        at = k * S + t * P
                        ins = pe.transpose(ps[:, bank + at // COLS, at % COLS:at % COLS + P],
                                           src[:, t * COLS + k * P:t * COLS + (k + 1) * P], ident[:, :])
                ins.then_inc(done, count)

            def turn_xn(stage_no, src):
                for q in range(PIECES):
                    pe.wait_ge(xn_ready, PIECES * stage_no + q + 1)
                    for k in range(2):
                        for t in range(TB):
                            ins = pe.transpose(ps[:, q, k * S + t * P:k * S + (t + 1) * P],
                                               src[:, t, (2 * q + k) * P:(2 * q + k + 1) * P], ident[:, :])
                    ins.then_inc(xn_turned, 1)

            def first_chunk(g, stage_no, inner=None):
                for j in range(IN_SUBS):
                    pe.wait_ge(y_lo, PIECES * stage_no + j + 1)
                    multiply(g + j, j, 0, 2 * j, act_hi, act_lo, j == 0, j == IN_SUBS - 1)

            pe.wait_ge(consts_made, 2)
            turn_xn(0, xn_h)
            pe.wait_ge(x_kept, 1)
            pe.wait_ge(small_landed, 16 * SMALLS)
            pe.transpose(ps[:, 0, 0:112], rowsA, ident[0:112, 0:112])
            pe.transpose(ps[:, 0, 128:224], rowsB, ident[0:96, 0:96]).then_inc(rows_turned, 1)
            pe.wait_ge(x_kept, PIECES)
            pe.wait_ge(cols_ready, 1)
            for o in range(N_OUT):
                pe.wait_ge(unit_added, (o + 1) * UNITS)
                for b in range(8):
                    ins = pe.matmul(ps[:, 4, 8 * o + b:8 * o + b + 1], head_acc[:, o, b * P:(b + 1) * P],
                                    ones[:, :], start=True, stop=True)
                ins.then_inc(job_summed, 1)
                for i in range(HEAD_SUBS):
                    g, k = HEAD_SUBS * o + i, 2 * o + i % 2
                    if i < 2:
                        pe.wait_ge(y_lo, k + 1)
                    multiply(g, g, HEAD_CHUNKS[i // 2][1], 2 * k, act_hi, act_lo, k == 0, k == PIECES - 1)

            def ffn(f):
                g0, t0, l0 = G_FFN[f], T_FFN[f], L_FFN[f]

                def pair(i, carried=False):
                    g = g0 + IN_SUBS + i * (2 * IN_SUBS)
                    if carried:
                        pe.wait_ge(tm_written, 1)
                    for j in range(IN_SUBS):
                        multiply(g + j, j, 2, 2 * j, act_hi, act_lo, j == 0, j == IN_SUBS - 1)
                        if carried and j == 0:
                            turn(tm, 4, turned)
                    pe.wait_ge(silu_done, PAIRS * f + 1 + i)
                    for j in range(IN_SUBS):
                        multiply(g + IN_SUBS + j, j, 0, 2 * j, act_hi, act_lo, j == 0, j == IN_SUBS - 1)
                        if j == 1:
                            pe.wait_ge(tm_written, t0 + 1 + i)
                            turn(tm, 4, turned)

                if f:
                    turn_xn(2, xn)
                    first_chunk(g0, 2)
                    pair(0)
                pair(1, carried=(f == 0))
                with pe.Fori(2, PAIRS - 1) as i:
                    pair(i)
                g = g0 + IN_SUBS * (2 * PAIRS - 1)
                for j in range(IN_SUBS):
                    multiply(g + j, j, 2, 2 * j, act_hi, act_lo, j == 0, j == IN_SUBS - 1)
                g += IN_SUBS
                for i in range(N_OUT * OUT_SUBS):
                    n, j = divmod(i, OUT_SUBS)
                    if i == 0:
                        pe.wait_ge(silu_done, PAIRS * (f + 1))
                        pe.wait_ge(turn_lo, l0 + PAIRS - 1)
                    if j == 0 and n >= 2:
                        pe.wait_ge(resid_added, TB * (R_FFN[f] + n - 1))
                    if i == OUT_SUBS - 2:
                        pe.wait_ge(turn_lo, l0 + PAIRS)
                    multiply(g + i, i, 2 * (n % 2), 2 * j, hid_hi, hid_lo, j == 0, j == OUT_SUBS - 1)
                    if i == 1:
                        pe.wait_ge(tm_written, t0 + PAIRS)
                        turn(tm, 4, turned)

            ffn(0)

            turn_xn(1, xn)
            first_chunk(G_MIX, 1)
            for ch in range(1, PROJ):
                for j in range(IN_SUBS):
                    i = ch * IN_SUBS + j
                    multiply(G_MIX + i, i, 2 * (ch % 2), 2 * j, act_hi, act_lo, j == 0, j == IN_SUBS - 1)
                    if j == 1 and ch <= 8:
                        pe.wait_ge(tm_written, T_MIX + ch)
                        if ch > 1:
                            pe.wait_ge(turn_kept, ch - 1)
                        turn(tm, 4, turned)
                    if ch == 4:
                        if j == 0:
                            pe.wait_ge(lru_w_landed, 32)
                        if j in (0, 4):
                            pe.wait_ge(conv_done, 1 + j // 4)
                        if j >= 2:
                            pe.wait_ge(gates_done, j - 1)
                        pe.matmul(ps[:, 6 + j % 2, 0:S], w_gate_r[:, j, :], xc[:, j, :], start=True, stop=True)
                        pe.matmul(ps[:, 6 + j % 2, S:2 * S], w_gate_i[:, j, :], xc[:, j, :],
                                  start=True, stop=True).then_inc(gates_summed, 1)

            def gate_chunk(cc, g, s):
                pe.wait_ge(kept, cc + 1)
                for j in range(IN_SUBS):
                    multiply(g + j, j, s, 2 * j, act_hi, act_lo, j == 0, j == IN_SUBS - 1)
                    if j == 0:
                        pe.wait_ge(head_fetched, cc * 2 + 2)
                        z = ps[:, 6, 0:3 * P]
                        k_one = k_t[:, bass.ds(cc, 1), :].rearrange("p a s -> p (a s)")
                        pe.matmul(z, ident_bf[:, :], bar[:, :], start=True, stop=False)
                        pe.matmul(z[:, 0:P], q_one[:, 0:P], k_one[:, 0:P], start=False, stop=False)
                        pe.matmul(z[:, P:3 * P], q_one[:, P:2 * P], k_one, start=False, stop=True).then_inc(scores, 1)
                    if j == 3:
                        pe.wait_ge(weights_ready, cc + 1)
                        for b in range(3):
                            ins = pe.transpose(ps[:, 4, b * P:(b + 1) * P], tm[:, COLS + b * P:COLS + (b + 1) * P], ident[:, :])
                        ins.then_inc(weights_turned, 1)
                    if j == 5:
                        pe.wait_ge(weights_kept, cc + 1)
                        pe.matmul(ps[:, 5, 0:P], v_one[:, 0, :], w_turned[:, 0:P], start=True, stop=True)
                        pe.matmul(ps[:, 5, P:2 * P], v_one[:, 0, :], w_turned[:, P:2 * P], start=True, stop=False)
                        pe.matmul(ps[:, 5, P:2 * P], v_one[:, 1, :], w_turned[:, 2 * P:3 * P],
                                  start=False, stop=True).then_inc(head_out, 1)

            gate_chunk(0, G_GATES, 0)
            with pe.Fori(0, (GATES - 2) // 2) as b:
                for half in range(2):
                    gate_chunk(b * 2 + 1 + half, G_GATES + IN_SUBS * (1 + half) + b * (2 * IN_SUBS), 2 - 2 * half)
            gate_chunk(GATES - 1, G_GATES + IN_SUBS * (GATES - 1), 2)

            pe.wait_ge(kept, 9)
            pe.wait_ge(attn_split, HEADS)
            for j in range(BR_SUBS):
                multiply(G_BR + j, j, 0, 2 * j, yat_hi, yat_lo, j == 0, j == BR_SUBS - 1)
            with pe.Fori(0, N_OUT - 1) as n:
                g = G_BR + BR_SUBS + n * (2 * BR_SUBS)
                pe.wait_ge(kept, 10)
                for j in range(BR_SUBS):
                    multiply(g + j, j, 2, 2 * j, ylru_hi, ylru_lo, j == 0, j == BR_SUBS - 1)
                pe.wait_ge(attn_merged, n + 1)
                for j in range(BR_SUBS):
                    multiply(g + BR_SUBS + j, j, 0, 2 * j, yat_hi, yat_lo, j == 0, j == BR_SUBS - 1)
                    if j == 0:
                        pe.wait_ge(tm_written, T_BR + 1 + n)
                        turn(tm, 4, turned)
            for j in range(BR_SUBS):
                multiply(G_OUT - BR_SUBS + j, j, 2, 2 * j, ylru_hi, ylru_lo, j == 0, j == BR_SUBS - 1)
            for i in range(N_OUT * IN_SUBS):
                n, j = divmod(i, IN_SUBS)
                if i == 0:
                    pe.wait_ge(attn_merged, N_OUT)
                    pe.wait_ge(turn_lo, L_BR + N_OUT - 1)
                if j == 0 and n >= 2:
                    pe.wait_ge(resid_added, TB * (R_OUT + n - 1))
                if i == IN_SUBS - 2:
                    pe.wait_ge(turn_lo, L_BR + N_OUT)
                multiply(G_OUT + i, i, 2 * (n % 2), 2 * j, act_hi, act_lo, j == 0, j == IN_SUBS - 1)
                if i == 1:
                    pe.wait_ge(tm_written, T_BR + N_OUT)
                    turn(tm, 4, turned)
            ffn(1)


_INS = ["x", "c", "w_ada", "b_ada", "norm_ffn1", "w_ffn1_in", "w_ffn1_out", "norm_mix", "w_in",
        "conv_w", "conv_b", "w_rg_gate", "b_rg_gate", "w_in_gate", "b_in_gate", "lru_lambda",
        "w_branch_attn", "w_branch_lru", "w_out", "norm_ffn2", "w_ffn2_in", "w_ffn2_out", "norm_final"]


def kernel(**inputs):
    import numpy as _np
    import concourse.bacc as _bacc
    from concourse import mybir as _mybir
    from concourse.bass_utils import run_bass_kernel_spmd as _run

    nc = _bacc.Bacc("TRN2", target_bir_lowering=False, num_devices=1, dynamic_dma_scratch_size=1024)
    arrays, args = {}, []
    for name in _INS:
        a = _np.ascontiguousarray(inputs[name])
        arrays[f"in_{name}_dram"] = a
        args.append(nc.dram_tensor(f"in_{name}_dram", a.shape, _mybir.dt.from_np(a.dtype), kind="ExternalInput").ap())
    shape = _np.asarray(inputs["x"]).shape
    args.append(nc.dram_tensor("out_0_dram", shape, _mybir.dt.float32, kind="ExternalOutput").ap())
    macaron_layer(nc, *args)
    r = _run(nc, [arrays], core_ids=[0])
    return r.results[0]["out_0_dram"]
```
